# Optimizing a Trainium2 kernel written in Bass

```python
import math
import jax, jax.numpy as jnp
from jax import lax
import numpy as np

D_MODEL = 1024
BATCH = 1
SEQ = 512
DEPTH = 1

MIX_WIDTH = D_MODEL
ATTN_WIDTH = MIX_WIDTH // 2
SSM_WIDTH = MIX_WIDTH - ATTN_WIDTH
HEAD_DIM = 64
N_HEADS = ATTN_WIDTH // HEAD_DIM
DILATED_BRANCHES = ((128, 1), (512, 4), (2048, 16))
BLOCK = 128
SSM_GROUP = 16
N_SSM_GROUPS = SSM_WIDTH // SSM_GROUP
STATE_DIM = 64
D_FF = 2816
IN_WIDTH = 3 * ATTN_WIDTH + SSM_WIDTH
NORM_EPS = 1e-6
DT_MIN = 1e-3
DT_MAX = 1e-1


def rms_norm(x, g):
    xf = x.astype(jnp.float32)
    y = xf * lax.rsqrt(jnp.mean(xf * xf, axis=-1, keepdims=True) + NORM_EPS)
    return (y * g.astype(jnp.float32)).astype(x.dtype)

def swiglu(x, w_in, w_out):
    gate, up = jnp.split(x @ w_in, 2, axis=-1)
    return (jax.nn.silu(gate) * up) @ w_out

def alibi_slopes(n_heads):
    return 2.0 ** (-8.0 * jnp.arange(1, n_heads + 1, dtype=jnp.float32) / n_heads)

def dilated_window_branch(q, k, v, slopes, window, dilation):
    B, S, H, E = q.shape
    n_back = window // dilation
    L = -(-S // dilation)
    nb = -(-L // BLOCK)
    Lp = nb * BLOCK

    def to_blocks(t):
        t = jnp.pad(t, ((0, 0), (0, L * dilation - S), (0, 0), (0, 0)))
        t = t.reshape(B, L, dilation, H, E).transpose(0, 2, 1, 3, 4)
        t = jnp.pad(t, ((0, 0), (0, 0), (0, Lp - L), (0, 0), (0, 0)))
        return t.reshape(B, dilation, nb, BLOCK, H, E)

    def with_prev(t):
        prev = jnp.pad(t[:, :, :-1], ((0, 0), (0, 0), (1, 0), (0, 0), (0, 0), (0, 0)))
        return jnp.concatenate([prev, t], axis=3)

    def from_blocks(t):
        tail = t.shape[4:]
        t = t.reshape((B, dilation, Lp) + tail)[:, :, :L]
        t = jnp.moveaxis(t, 1, 2).reshape((B, L * dilation) + tail)
        return t[:, :S]

    qb, kb, vb = to_blocks(q), to_blocks(k), to_blocks(v)
    kk, vv = with_prev(kb), with_prev(vb)
    s = jnp.einsum('brnqhe,brnkhe->brnhqk', qb, kk) * (HEAD_DIM ** -0.5)

    qi = jnp.arange(BLOCK)[:, None]
    ci = jnp.arange(2 * BLOCK)[None, :]
    steps = BLOCK + qi - ci
    key_pos = (jnp.arange(nb)[:, None, None] - 1) * BLOCK + ci[None]
    valid = ((steps >= 0) & (steps <= n_back))[None] & (key_pos >= 0)
    dist = (steps * dilation).astype(jnp.float32)
    bias = -slopes[:, None, None] * dist[None]
    s = jnp.where(valid[None, None, :, None], s + bias, -jnp.inf)

    m = jnp.max(s, axis=-1, keepdims=True)
    p = jnp.exp(s - m)
    denom = jnp.sum(p, axis=-1, keepdims=True)
    o = jnp.einsum('brnhqk,brnkhe->brnqhe', p, vv)
    o = o * jnp.swapaxes(1.0 / denom[..., 0], -1, -2)[..., None]
    lse = jnp.swapaxes((m + jnp.log(denom))[..., 0], -1, -2)
    return from_blocks(o), from_blocks(lse)

def dilated_attention(q, k, v):
    B, S, _ = q.shape
    q, k, v = (t.astype(jnp.float32).reshape(B, S, N_HEADS, HEAD_DIM) for t in (q, k, v))
    slopes = alibi_slopes(N_HEADS)
    outs, lses = [], []
    for window, dilation in DILATED_BRANCHES:
        o, l = dilated_window_branch(q, k, v, slopes, window, dilation)
        outs.append(o)
        lses.append(l)
    w = jax.nn.softmax(jnp.stack(lses, axis=-1), axis=-1)
    o = jnp.einsum('bshn,nbshe->bshe', w, jnp.stack(outs, axis=0))
    return o.reshape(B, S, ATTN_WIDTH)

def s5_mixer(u, a_re, a_im, log_dt, b_re, b_im, c_re, c_im, d_skip, w_glu, b_glu):
    B, S, _ = u.shape
    f32 = jnp.float32
    uf = u.astype(f32).reshape(B, S, N_SSM_GROUPS, SSM_GROUP)
    dt = jnp.exp(log_dt.astype(f32))[:, None]
    a = lax.complex(a_re.astype(f32), a_im.astype(f32))
    a_bar = jnp.exp(dt * a)
    b = lax.complex(b_re.astype(f32), b_im.astype(f32))
    b_bar = ((a_bar - 1.0) / a)[..., None] * b
    bu = jnp.einsum('bsgc,gpc->bsgp', uf.astype(jnp.complex64), b_bar)
    a_seq = jnp.broadcast_to(a_bar, bu.shape)

    def combine(left, right):
        a_l, x_l = left
        a_r, x_r = right
        return a_r * a_l, a_r * x_l + x_r

    _, states = lax.associative_scan(combine, (a_seq, bu), axis=1)
    c = lax.complex(c_re.astype(f32), c_im.astype(f32))
    y = jnp.real(jnp.einsum('bsgp,gcp->bsgc', states, c))
    y = y + d_skip.astype(f32).reshape(N_SSM_GROUPS, SSM_GROUP) * uf
    y = jax.nn.gelu(y.reshape(B, S, SSM_WIDTH))
    return y * jax.nn.sigmoid(y @ w_glu.astype(f32) + b_glu.astype(f32))

def first_inputs(seed: int = 0) -> dict:
    key = jax.random.key(seed)
    ks = jax.random.split(key, 24)
    f32 = jnp.float32
    L = DEPTH

    def nrm(k, shape, scale):
        return jax.random.normal(k, shape, f32) * scale

    def gain(k):
        return 1.0 + 0.05 * jax.random.normal(k, (L, D_MODEL), f32)

    n_idx = jnp.arange(STATE_DIM, dtype=f32)
    a_re = -0.5 + 0.01 * jax.random.normal(ks[9], (L, N_SSM_GROUPS, STATE_DIM), f32)
    a_im = math.pi * n_idx + 0.01 * jax.random.normal(ks[10], (L, N_SSM_GROUPS, STATE_DIM), f32)
    log_dt = jax.random.uniform(ks[11], (L, N_SSM_GROUPS), f32,
                                math.log(DT_MIN), math.log(DT_MAX))
    return {
        "x": jax.random.normal(ks[0], (BATCH, SEQ, D_MODEL), f32),
        "ffn1_pre_g": gain(ks[1]),
        "ffn1_w_in": nrm(ks[2], (L, D_MODEL, 2 * D_FF), D_MODEL ** -0.5),
        "ffn1_w_out": nrm(ks[3], (L, D_FF, D_MODEL), D_FF ** -0.5),
        "ffn1_post_g": gain(ks[4]),
        "mix_pre_g": gain(ks[5]),
        "w_mix_in": nrm(ks[6], (L, D_MODEL, IN_WIDTH), D_MODEL ** -0.5),
        "a_re": a_re,
        "a_im": a_im,
        "log_dt": log_dt,
        "b_re": nrm(ks[12], (L, N_SSM_GROUPS, STATE_DIM, SSM_GROUP), (2 * SSM_GROUP) ** -0.5),
        "b_im": nrm(ks[13], (L, N_SSM_GROUPS, STATE_DIM, SSM_GROUP), (2 * SSM_GROUP) ** -0.5),
        "c_re": nrm(ks[14], (L, N_SSM_GROUPS, SSM_GROUP, STATE_DIM), (2 * STATE_DIM) ** -0.5),
        "c_im": nrm(ks[15], (L, N_SSM_GROUPS, SSM_GROUP, STATE_DIM), (2 * STATE_DIM) ** -0.5),
        "d_skip": nrm(ks[16], (L, SSM_WIDTH), 1.0),
        "w_glu": nrm(ks[17], (L, SSM_WIDTH, SSM_WIDTH), SSM_WIDTH ** -0.5),
        "b_glu": nrm(ks[18], (L, SSM_WIDTH), 0.01),
        "w_mix_out": nrm(ks[19], (L, MIX_WIDTH, D_MODEL), MIX_WIDTH ** -0.5),
        "mix_post_g": gain(ks[20]),
        "ffn2_pre_g": gain(ks[21]),
        "ffn2_w_in": nrm(ks[22], (L, D_MODEL, 2 * D_FF), D_MODEL ** -0.5),
        "ffn2_w_out": nrm(ks[23], (L, D_FF, D_MODEL), D_FF ** -0.5),
        "ffn2_post_g": gain(ks[7]),
    }

def first_block(x, ffn1_pre_g, ffn1_w_in, ffn1_w_out, ffn1_post_g, mix_pre_g, w_mix_in,
              a_re, a_im, log_dt, b_re, b_im, c_re, c_im, d_skip, w_glu, b_glu,
              w_mix_out, mix_post_g, ffn2_pre_g, ffn2_w_in, ffn2_w_out, ffn2_post_g):
    for l in range(DEPTH):
        h = rms_norm(x, ffn1_pre_g[l])
        x = x + 0.5 * rms_norm(swiglu(h, ffn1_w_in[l], ffn1_w_out[l]), ffn1_post_g[l])
        h = rms_norm(x, mix_pre_g[l])
        proj = h @ w_mix_in[l]
        q, k, v, u = jnp.split(proj, [ATTN_WIDTH, 2 * ATTN_WIDTH, 3 * ATTN_WIDTH], axis=-1)
        attn = dilated_attention(q, k, v).astype(x.dtype)
        ssm = s5_mixer(u, a_re[l], a_im[l], log_dt[l], b_re[l], b_im[l], c_re[l], c_im[l],
                       d_skip[l], w_glu[l], b_glu[l]).astype(x.dtype)
        mixed = jnp.concatenate([attn, ssm], axis=-1) @ w_mix_out[l]
        x = x + rms_norm(mixed, mix_post_g[l])
        h = rms_norm(x, ffn2_pre_g[l])
        x = x + 0.5 * rms_norm(swiglu(h, ffn2_w_in[l], ffn2_w_out[l]), ffn2_post_g[l])
    return x


DEPTH_2 = 2

D_MIX = D_MODEL
D_POOL = D_MIX // 2
D_HGRN = D_MIX - D_POOL
POOL_WINDOWS = (2, 4, 8, 16)
N_POOL_GROUPS = len(POOL_WINDOWS)
POOL_GROUP_DIM = D_POOL // N_POOL_GROUPS
HGRN_HEADS = 4
HGRN_HEAD_DIM = D_HGRN // HGRN_HEADS
CHUNK = 64
D_IN = D_POOL + 4 * D_HGRN
D_FF_2 = ((8 * D_MODEL // 3 + 127) // 128) * 128
ALPHA = (2.0 * DEPTH_2) ** 0.25
BETA = (8.0 * DEPTH_2) ** -0.25
LN_EPS = 1e-5
RMS_EPS = 1e-6


def layer_norm(x, g, b):
    x32 = x.astype(jnp.float32)
    mu = jnp.mean(x32, axis=-1, keepdims=True)
    var = jnp.mean(jnp.square(x32 - mu), axis=-1, keepdims=True)
    y = (x32 - mu) * lax.rsqrt(var + LN_EPS) * g.astype(jnp.float32) + b.astype(jnp.float32)
    return y.astype(x.dtype)

def swiglu_2(x, w_gate, w_up, w_down):
    return (jax.nn.silu(x @ w_gate) * (x @ w_up)) @ w_down

def multiscale_pool(u, pool_w, pool_scale):
    B, S, _ = u.shape
    u32 = u.astype(jnp.float32).reshape(B, S, N_POOL_GROUPS, POOL_GROUP_DIM)
    c = jnp.cumsum(u32, axis=1)
    pos = jnp.arange(S)
    means = []
    for g, w in enumerate(POOL_WINDOWS):
        cg = c[:, :, g]
        lag = jnp.pad(cg, ((0, 0), (w, 0), (0, 0)))[:, :S]
        cnt = jnp.minimum(pos + 1, w).astype(jnp.float32)[None, :, None]
        means.append((cg - lag) / cnt)
    pooled = jnp.stack(means, axis=2) - u32
    y = jnp.einsum('bsgc,gcd->bsgd', pooled.astype(u.dtype), pool_w)
    return y.reshape(B, S, D_POOL) * pool_scale

def hgrn2_recurrence(q, f_raw, v, lb):
    B, S, _ = q.shape
    n = S // CHUNK
    log_f = jnp.logaddexp(jnp.log(lb), jnp.log1p(-lb) + jax.nn.log_sigmoid(f_raw))
    k = (1.0 - lb) * jax.nn.sigmoid(-f_raw)
    q = q * (HGRN_HEAD_DIM ** -0.5)

    def heads(t):
        return t.reshape(B, n, CHUNK, HGRN_HEADS, HGRN_HEAD_DIM).transpose(1, 0, 3, 2, 4)

    causal = jnp.tril(jnp.ones((CHUNK, CHUNK), dtype=bool))[:, :, None]

    def step(state, inp):
        q_c, k_c, v_c, g_c = inp
        b = jnp.cumsum(g_c, axis=2)
        o_inter = jnp.einsum('bhtd,bhdv->bhtv', q_c * jnp.exp(b), state)
        rel = b[:, :, :, None, :] - b[:, :, None, :, :]
        decay = jnp.exp(jnp.where(causal, rel, -jnp.inf))
        scores = jnp.einsum('bhtd,bhsd,bhtsd->bhts', q_c, k_c, decay)
        o_intra = jnp.einsum('bhts,bhsv->bhtv', scores, v_c)
        b_last = b[:, :, -1:, :]
        k_dec = k_c * jnp.exp(b_last - b)
        new_state = jnp.exp(b_last[:, :, 0, :])[..., None] * state + jnp.einsum('bhsd,bhsv->bhdv', k_dec, v_c)
        return new_state, o_inter + o_intra

    s0 = jnp.zeros((B, HGRN_HEADS, HGRN_HEAD_DIM, HGRN_HEAD_DIM), jnp.float32)
    _, o = lax.scan(step, s0, (heads(q), heads(k), heads(v), heads(log_f)))
    return o.transpose(1, 0, 3, 2, 4).reshape(B, S, D_HGRN)

def head_rms_norm(o, g):
    B, S, _ = o.shape
    o = o.reshape(B, S, HGRN_HEADS, HGRN_HEAD_DIM)
    o = o * lax.rsqrt(jnp.mean(jnp.square(o), axis=-1, keepdims=True) + RMS_EPS) * g.astype(jnp.float32)
    return o.reshape(B, S, D_HGRN)

def second_inputs(seed: int = 0) -> dict:
    key = jax.random.key(seed)
    ks = jax.random.split(key, 16)
    nrm = jax.random.normal
    f32 = jnp.float32
    x = nrm(ks[0], (BATCH, SEQ, D_MODEL), f32)
    w_in = nrm(ks[1], (DEPTH_2, D_MODEL, D_IN), f32) * D_MODEL ** -0.5
    pool_w = nrm(ks[2], (DEPTH_2, N_POOL_GROUPS, POOL_GROUP_DIM, POOL_GROUP_DIM), f32) * POOL_GROUP_DIM ** -0.5
    pool_scale = 1.0 + 0.02 * nrm(ks[3], (DEPTH_2, D_POOL), f32)
    lb_param = 0.5 * nrm(ks[4], (DEPTH_2, D_HGRN), f32)
    hgrn_norm_g = 1.0 + 0.02 * nrm(ks[5], (DEPTH_2, HGRN_HEAD_DIM), f32)
    w_out = nrm(ks[6], (DEPTH_2, D_MIX, D_MODEL), f32) * (D_MIX ** -0.5 * BETA)
    ffn1_gate = nrm(ks[7], (DEPTH_2, D_MODEL, D_FF_2), f32) * D_MODEL ** -0.5
    ffn1_up = nrm(ks[8], (DEPTH_2, D_MODEL, D_FF_2), f32) * D_MODEL ** -0.5
    ffn1_down = nrm(ks[9], (DEPTH_2, D_FF_2, D_MODEL), f32) * (D_FF_2 ** -0.5 * BETA)
    ffn2_gate = nrm(ks[10], (DEPTH_2, D_MODEL, D_FF_2), f32) * D_MODEL ** -0.5
    ffn2_up = nrm(ks[11], (DEPTH_2, D_MODEL, D_FF_2), f32) * D_MODEL ** -0.5
    ffn2_down = nrm(ks[12], (DEPTH_2, D_FF_2, D_MODEL), f32) * (D_FF_2 ** -0.5 * BETA)
    ln_g = 1.0 + 0.02 * nrm(ks[13], (DEPTH_2, 3, D_MODEL), f32)
    ln_b = 0.02 * nrm(ks[14], (DEPTH_2, 3, D_MODEL), f32)
    return {"x": x, "w_in": w_in, "pool_w": pool_w, "pool_scale": pool_scale, "lb_param": lb_param,
            "hgrn_norm_g": hgrn_norm_g, "w_out": w_out, "ffn1_gate": ffn1_gate, "ffn1_up": ffn1_up,
            "ffn1_down": ffn1_down, "ffn2_gate": ffn2_gate, "ffn2_up": ffn2_up, "ffn2_down": ffn2_down,
            "ln_g": ln_g, "ln_b": ln_b}

def second_block(x, w_in, pool_w, pool_scale, lb_param, hgrn_norm_g, w_out, ffn1_gate, ffn1_up, ffn1_down,
              ffn2_gate, ffn2_up, ffn2_down, ln_g, ln_b):
    f32 = jnp.float32
    lb_all = jnp.cumsum(jax.nn.softmax(lb_param.astype(f32), axis=0), axis=0)
    lb_all = lb_all - lb_all[0:1]
    for l in range(DEPTH_2):
        x = layer_norm(ALPHA * x + 0.5 * swiglu_2(x, ffn1_gate[l], ffn1_up[l], ffn1_down[l]), ln_g[l, 0], ln_b[l, 0])
        h = x @ w_in[l]
        u = h[..., :D_POOL]
        q, f_raw, v, g = jnp.split(h[..., D_POOL:], 4, axis=-1)
        y_pool = multiscale_pool(u, pool_w[l], pool_scale[l])
        o = hgrn2_recurrence(q.astype(f32), f_raw.astype(f32), v.astype(f32), lb_all[l])
        y_hgrn = head_rms_norm(o, hgrn_norm_g[l]) * jax.nn.silu(g.astype(f32))
        mix = jnp.concatenate([y_pool.astype(x.dtype), y_hgrn.astype(x.dtype)], axis=-1) @ w_out[l]
        x = layer_norm(ALPHA * x + mix, ln_g[l, 1], ln_b[l, 1])
        x = layer_norm(ALPHA * x + 0.5 * swiglu_2(x, ffn2_gate[l], ffn2_up[l], ffn2_down[l]), ln_g[l, 2], ln_b[l, 2])
    return x


def setup_inputs(seed=0):
    out = dict(first_inputs(seed))
    for name, value in second_inputs(seed + 1).items():
        if name != "x":
            out[name + "_2"] = value
    return out


def reference(
    x, ffn1_pre_g, ffn1_w_in, ffn1_w_out, ffn1_post_g, mix_pre_g, w_mix_in, a_re, a_im, log_dt,
    b_re, b_im, c_re, c_im, d_skip, w_glu, b_glu, w_mix_out, mix_post_g, ffn2_pre_g, ffn2_w_in,
    ffn2_w_out, ffn2_post_g, w_in_2, pool_w_2, pool_scale_2, lb_param_2, hgrn_norm_g_2, w_out_2,
    ffn1_gate_2, ffn1_up_2, ffn1_down_2, ffn2_gate_2, ffn2_up_2, ffn2_down_2, ln_g_2, ln_b_2,
):
    x = first_block(
        x, ffn1_pre_g, ffn1_w_in, ffn1_w_out, ffn1_post_g, mix_pre_g, w_mix_in, a_re, a_im,
        log_dt, b_re, b_im, c_re, c_im, d_skip, w_glu, b_glu, w_mix_out, mix_post_g, ffn2_pre_g,
        ffn2_w_in, ffn2_w_out, ffn2_post_g,
    )
    return second_block(
        x, w_in_2, pool_w_2, pool_scale_2, lb_param_2, hgrn_norm_g_2, w_out_2, ffn1_gate_2,
        ffn1_up_2, ffn1_down_2, ffn2_gate_2, ffn2_up_2, ffn2_down_2, ln_g_2, ln_b_2,
    )


_drawn_inputs = setup_inputs


def setup_inputs(seed=0):
    import zlib

    import numpy as np

    out = dict(_drawn_inputs(seed))
    spreads = {}
    factors = {'a_re': 64.0,
     'b_glu': 8.0,
     'ffn2_post_g': 3.235,
     'pool_scale_2': 8.0,
     'hgrn_norm_g_2': 24.543,
     'b_re': 2.845,
     'b_im': 2.882,
     'c_re': 2.846,
     'c_im': 2.725}
    for name, (base, spread) in spreads.items():
        noise = np.random.default_rng([zlib.crc32(name.encode()), seed]).standard_normal(out[name].shape)
        drawn = base * np.exp(spread * noise) if base else spread * noise
        out[name] = __import__('jax').numpy.asarray(drawn.astype(out[name].dtype))
    for name, factor in factors.items():
        out[name] = (out[name] * factor).astype(out[name].dtype)
    return out
```

```python
import math

import concourse.bass as bass
from concourse import mybir

P = 128
T = 512
D = 1024
KD = D // P
NF = 2816 // P
F32 = mybir.dt.float32
F32R = mybir.dt.float32r
U8 = mybir.dt.uint8
ALU = mybir.AluOpType
ACT = mybir.ActivationFunctionType
AX_X = mybir.AxisListType.X
MUL, ADD, SUB = ALU.mult, ALU.add, ALU.subtract

ALPHA = 4.0 ** 0.25
NR = 3
NH = 3
AHEAD = 2
HEADS = 8
LEVELS = (0, 1, 2, 4, 8, 16, 32, 64)

COLS = {}
_at = 0
for _name, _n in (("ident", 128), ("g_f1pre", 8), ("g_f1post", 8), ("g_mpre", 8), ("g_mpost", 8),
                  ("g_f2pre", 8), ("g_f2post", 8), ("ln_g", 48), ("ln_b", 48), ("pool_scale", 8),
                  ("lb", 8), ("hg", 2), ("b_glu", 4), ("a_re", 16), ("a_im", 16), ("log_dt", 16),
                  ("d_skip", 32), ("rcount", 64)):
    COLS[_name] = (_at, _at + _n)
    _at += _n
NCOLS = _at


def stream_plan():
    plan = []

    def groups(name, cols):
        for k in range(KD):
            plan.extend((n, k, c) for n, c in zip(name, cols))

    def rows(name, nk, nn):
        plan.extend((name, k, c) for c in range(nn) for k in range(nk))

    def ffn_in(gate, up, base):
        for j in range(0, NF, 2):
            groups((gate, gate, up, up), (j, j + 1, base + j, base + j + 1))

    ffn_in("f1_in", "f1_in", NF)
    rows("f1_out", NF, KD)
    for c in (12, 0, 4, 8):
        groups(("mix_in",) * 4, range(c, c + 4))
    rows("glu", 4, 4)
    rows("mix_out", KD, KD)
    ffn_in("f2_in", "f2_in", NF)
    rows("f2_out", NF, KD)
    for l in range(2):
        ffn_in(f"gate1_{l}", f"up1_{l}", 0)
        rows(f"down1_{l}", NF, KD)
        for c in (8, 4, 12, 0, 16):
            groups((f"in_{l}",) * 4, range(c, c + 4))
        plan.extend((f"pool{g}_{l}", 0, 0) for g in range(4))
        rows(f"out_{l}", KD, KD)
        ffn_in(f"gate2_{l}", f"up2_{l}", 0)
        rows(f"down2_{l}", NF, KD)
    return plan


class Queue:

    def __init__(self, sem):
        self.sem = sem
        self.ops = []
        self.n = 0

    def __call__(self, fn, *waits, sig=True):
        self.ops.append((waits, fn, sig))
        if not sig:
            return None
        self.n += 1
        return (self.sem, self.n)


def flat(waits):
    for w in waits:
        if w is None:
            continue
        if isinstance(w, list):
            yield from flat(w)
        else:
            yield w


def run_queue(eng, queue):
    seen = {}
    for waits, fn, sig in queue.ops:
        need = {}
        for sem, value in flat(waits):
            if value > max(seen.get(id(sem), 0), need.get(id(sem), (None, 0))[1]):
                need[id(sem)] = (sem, value)
        for key, (sem, value) in need.items():
            eng.wait_ge(sem, value)
            seen[key] = value
        ins = fn(eng)
        if sig is True:
            ins.then_inc(queue.sem, 1)
        elif sig:
            ins.then_inc(sig, 16)


def build(nc, x_d, w_d, cst_d, s5_d, att_d, msk_d, out_d, taps=None):
    n_units = w_d.shape[0]
    sem = {n: nc.alloc_semaphore(n) for n in ("pe", "act", "dve", "pool", "s_cst", "s_s5", "s_att", "s_msk",
                                              "s_w3", "s_out")}
    ds = [nc.alloc_semaphore(f"ds{i}") for i in range(NR)]
    dx = [nc.alloc_semaphore(f"dx{i}") for i in range(4)]
    pe, act, dve, pool = (Queue(sem[n]) for n in ("pe", "act", "dve", "pool"))
    sp = Queue(None)

    top = [1152]

    def at(name, shape, dt, offset=None):
        size = math.prod(shape[1:]) * (1 if dt == U8 else 4)
        if offset is None:
            offset = top[0]
            top[0] += (size + 31) // 32 * 32
        return nc.alloc_sbuf_tensor_at(name, list(shape), dt, offset=offset)

    X = at("X", [P, KD, T], F32)
    Hh = at("Hh", [P, KD, T], F32R)
    Hl = at("Hl", [P, KD, T], F32R)
    wraw = at("wraw", [P, NR, 1024], F32)
    whi = at("whi", [P, NH, 1024], F32R)
    wlo = at("wlo", [P, NH, 1024], F32R)
    cst = at("cst", [P, NCOLS], F32)
    msk = at("msk", [P, 8, P], U8)
    ones = at("ones", [P, P], F32)
    epsc = at("epsc", [P, 4], F32)
    gh = at("gh", [P, 16], F32)
    rcol = at("rcol", [P, 48], F32)
    hcol = at("hcol", [P, 32], F32)
    small = at("small", [P, 64], F32)
    acc = at("acc", [P, T], F32)
    zsum = at("zsum", [P, T], F32)
    Rb = at("Rb", [P, T], F32)
    MUb = at("MUb", [P, T], F32)
    tmp = [at(f"tmp{i}", [P, T], F32) for i in range(5)]
    dgt = at("dgt", [P, 4, P], F32)
    sq = at("sq", [P, T], F32)
    Bre = at("Bre", [P, 16, 16], F32)
    Bim = at("Bim", [P, 16, 16], F32)
    pw = at("pw", [P, 5, 9, 16], F32)
    sp5 = at("sp5", [P, 16, 16], F32)
    M8 = at("M8", [P, 2, 32], F32)
    arena = top[0]
    cur = [arena]

    def ar(name, shape, dt, offset=None):
        size = math.prod(shape[1:]) * 4
        if offset is None:
            offset = cur[0]
            cur[0] += size
        assert offset + size <= 229344, (name, offset + size)
        return nc.alloc_sbuf_tensor_at(name, list(shape), dt, offset=offset), offset

    Ah, _ = ar("Ah", [P, NF, T], F32R)
    Al, _ = ar("Al", [P, NF, T], F32R)
    Y, _ = ar("Y", [P, KD, T], F32)
    cur[0] = arena
    Qf, _ = ar("Qf", [P, 4, T], F32)
    Kf, _ = ar("Kf", [P, 4, T], F32)
    Vt, _ = ar("Vt", [P, 4, T], F32)
    PT, o_pt = ar("PT", [P, 4, T], F32)
    U2, o_u2 = ar("U2", [P, 32, 4, 16], F32)
    cur[0] += 8192
    Up, o_up = ar("Up", [P, 32, 64], F32)
    W1, o_w1 = ar("W1", [P, 16, 2, 2, 64], F32)
    Gre, _ = ar("Gre", [P, 16, 9, 16], F32)
    Gim, _ = ar("Gim", [P, 16, 9, 16], F32)
    Wri, o_wr = ar("Wri", [P, 2, 16, 8, 16], F32)
    W3, _ = ar("W3", [P, 32, P], F32, o_u2)
    yh, _ = ar("yh", [P, 4, T], F32R, o_u2)
    yl, _ = ar("yl", [P, 4, T], F32R, o_u2 + 8192)
    yg, _ = ar("yg", [P, 4, T], F32, o_up)
    Kr, _ = ar("Kr", [P, 32, P], F32, o_w1)
    Y2, _ = ar("Y2", [P, 8, T], F32, o_w1)
    FS, _ = ar("FS", [P, 64, 2, 16], F32, o_wr)
    XS, _ = ar("XS", [P, 64, 2, 16], F32, o_wr + 8192)
    Wt, _ = ar("Wt", [P, 16, 8, 16], F32, o_pt)
    Gt, _ = ar("Gt", [P, 16, 9, 16], F32, o_wr)
    cur[0] = arena
    QP, _ = ar("QP", [P, 4, T], F32)
    KS, _ = ar("KS", [P, 4, T], F32)
    FT, _ = ar("FT", [P, 4, T], F32)
    TT, _ = ar("TT", [P, 4 * T], F32)
    V2, _ = ar("V2", [P, 4, T], F32)
    Sc, _ = ar("Sc", [P, 4, 4, T], F32)
    Sg, _ = ar("Sg", [P, 4, T], F32)
    Oh, _ = ar("Oh", [P, 4, T], F32)
    U3, _ = ar("U3", [P, 4, 16 + T], F32)
    PA, _ = ar("PA", [P, 2, 16 + T], F32)
    Dp, Cn = zsum, MUb

    bank_t = [nc.alloc_psum_tensor(f"bank{i}", [P, T], F32) for i in range(8)]
    bfree = [[] for _ in range(8)]
    bnext = [0]

    def bank():
        while bfree[bnext[0] % 8] is None:
            bnext[0] += 1
        i = bnext[0] % 8
        bnext[0] += 1
        w = bfree[i]
        bfree[i] = None
        return i, bank_t[i], w

    def c(name, i=None, n=1):
        a, b = COLS[name]
        return cst[:, a:b] if i is None else cst[:, a + i:a + i + n]

    ident = c("ident")

    def mm(out, lhsT, rhs, start, stop, *waits, sig=False, skip=False):
        return pe(lambda e: e.matmul(out, lhsT, rhs, start=start, stop=stop, skip_group_check=skip),
                  *waits, sig=sig)

    def tr(out, in_, idn, *waits, sig=False):
        return pe(lambda e: e.transpose(out, in_, idn), *waits, sig=sig)

    def A(out, in_, func, *waits, **kw):
        return act(lambda e: e.activation(out, in_, func, **kw), *waits)

    def tt(q, out, a, b, op, *waits):
        return q(lambda e: e.tensor_tensor(out, a, b, op), *waits)

    def ts(q, out, a, s1, s2, op0, op1, *waits):
        if op1 is None:
            return q(lambda e: e.tensor_scalar(out, a, s1, None, op0), *waits)
        return q(lambda e: e.tensor_scalar(out, a, s1, s2, op0, op1), *waits)

    def stt(out, a, s, b, op0, op1, *waits, **kw):
        return dve(lambda e: e.scalar_tensor_tensor(out, a, s, b, op0, op1, **kw), *waits)

    def f32(ap):
        return ap.bitcast(F32)

    lo_done = {}
    unit_used = {}
    pos = [0]

    def load(u):
        if u < n_units:
            sp(lambda e: e.dma_start(wraw[:, u % NR, :], w_d[u]), lo_done.get(u - NR), sig=ds[u % NR])

    def prep(u):
        if u >= n_units:
            return
        r, h = u % NR, u % NH
        hi = A(whi[:, h, :], wraw[:, r, :], ACT.Copy, (ds[r], 16 * (u // NR + 1)), unit_used.get(u - NH))
        lo_done[u] = tt(dve, wlo[:, h, :], wraw[:, r, :], f32(whi[:, h, :]), SUB, hi)
        load(u + NR)

    def wtile(n=1):
        i = pos[0]
        u, t = i // 8, i % 8
        if t == 0:
            prep(u + AHEAD)
        pos[0] += n
        h = u % NH
        return whi[:, h, t * P:(t + n) * P], wlo[:, h, t * P:(t + n) * P], lo_done[u], (u if t + n == 8 else None)

    def mm3(out, sh, sl, mh, ml, start, stop, waits, unit, sig=False):
        mm(out, sh, mh, start, False, *waits)
        mm(out, sh, ml, False, False)
        t = mm(out, sl, mh, False, stop, sig=sig or unit is not None)
        if unit is not None:
            unit_used[unit] = t
        return t

    def gemm_group(mh, ml, hw):
        banks = [bank() for _ in range(4)]
        for k in range(KD):
            for i in range(4):
                hi, lo, w, unit = wtile()
                last = k == KD - 1
                t = mm3(banks[i][1][:, :], hi, lo, mh[:, k, :], ml[:, k, :], k == 0, last,
                        [w, hw[k], banks[i][2] if k == 0 else None], unit, sig=last and i == 3)
        return [b[0] for b in banks], t

    def gemm_tokens(toks, hw):
        banks = [bank() for _ in range(4)]
        for k in range(KD):
            hi, lo, w, unit = wtile(4)
            for m in range(4):
                out = banks[m][1][:, :]
                ww = [w, hw[k], banks[m][2] if k == 0 else None]
                mm(out, toks(Hh, k, m), hi, k == 0, False, *ww)
                mm(out, toks(Hl, k, m), hi, False, False)
                last = k == KD - 1
                t = mm(out, toks(Hh, k, m), lo, False, last, sig=m == 3 and (last or unit is not None))
            if unit is not None:
                unit_used[unit] = t
        return [b[0] for b in banks], t

    def gemm_row(nk, mh, ml, mw, mid=None):
        i, b, w0 = bank()
        for k in range(nk):
            hi, lo, w, unit = wtile()
            t = mm3(b[:, :], hi, lo, mh[:, k, :], ml[:, k, :], k == 0, k == nk - 1,
                    [w, mw[k], w0 if k == 0 else None], unit, sig=k == nk - 1)
            if mid is not None:
                mid(k)
        return i, t

    for k in range(0, KD, 2):
        sp(lambda e, k=k: e.dma_start(X[:, k:k + 2, :], x_d[:, k:k + 2, :]), sig=dx[k // 2])
        if k == 0:
            sp(lambda e: e.dma_start(cst[:, :], cst_d), sig=sem["s_cst"])
    for u in range(NR):
        load(u)
    sp(lambda e: e.dma_start(tmp[4][:, :], s5_d[:, 0, :]), sig=sem["s_s5"])
    sp(lambda e: e.dma_start(MUb[:, :], s5_d[:, 1, :]), sig=sem["s_s5"])
    sp(lambda e: e.dma_start(Y[:, 0:2, :], msk_d), sig=sem["s_msk"])
    cst_in = (sem["s_cst"], 16)
    ones_in = pool(lambda e: e.memset(ones[:, :], 1.0))
    pool(lambda e: e.memset(epsc[:, 0:1], 1e-6))
    pool(lambda e: e.memset(epsc[:, 1:2], 1e-5))
    eps_in = pool(lambda e: e.memset(epsc[:, 2:3], math.pi / 2))
    pd = {"act": [cst_in, eps_in], "dve": [cst_in]}
    gh_in = ts(dve, gh[:, 0:8], c("g_f1post"), 0.5, None, MUL, None, cst_in)
    gh_in = ts(dve, gh[:, 8:16], c("g_f2post"), 0.5, None, MUL, None, cst_in)
    prep(0)
    prep(1)
    msk_in = dve(lambda e: e.tensor_copy(msk[:, :, :].rearrange("p a b -> p (a b)"),
                                         Y[:, 0:2, :].rearrange("p a b -> p (a b)")), (sem["s_msk"], 16))

    state = {"x": [(dx[k // 2], 16) for k in range(KD)], "h_used": None, "acc_used": None, "zsum_used": None,
             "tmp": [None] * 5, "dg_used": None, "Rb_used": None, "MUb_used": None, "arena": None,
             "sq_used": None, "y_free": msk_in}

    def split_h(k, src, scale, ready):
        if scale is None:
            hi = A(Hh[:, k, :], src, ACT.Copy, ready, state["h_used"])
            lo = tt(dve, Hl[:, k, :], src, f32(Hh[:, k, :]), SUB, hi, ready, state["h_used"])
        else:
            hi = A(Hh[:, k, :], src, ACT.Copy, ready, state["h_used"], cst_in, scale=scale)
            lo = stt(Hl[:, k, :], src, scale, f32(Hh[:, k, :]), MUL, SUB, hi, ready, state["h_used"], cst_in)
        return [hi, lo]

    def add_square(src, first, ready):
        if first:
            t = tt(pool, acc[:, :], src, src, MUL, ready, state["acc_used"])
        else:
            s = tt(pool, sq[:, :], src, src, MUL, ready, state["sq_used"], state.get("acc"))
            t = tt(pool, acc[:, :], acc[:, :], sq[:, :], ADD, s)
        state["acc"] = t
        return t

    def col_sums(src, b, col, ready, w0, perm=False):
        for m in range(4):
            lhsT = src[:, m::4] if perm else src[:, m * P:(m + 1) * P]
            t = mm(b[:, col + 2 * m:col + 2 * m + 2], lhsT, ones[:, 0:2], True, True, ready, w0, ones_in,
                   sig=m == 3, skip=True)
        return t

    def spread(cols, ready, b, w0):
        for m in range(4):
            dg = ts(dve, dgt[:, m, :], ident, cols(m), None, MUL, None, ready, state["dg_used"], cst_in)
        for m in range(4):
            t = mm(b[:, m * P:(m + 1) * P], ones[:, :], dgt[:, m, :], True, True, dg, w0, sig=m == 3, skip=True)
        state["dg_used"] = t
        return t

    def rms_cols(ready, perm):
        i, b, w0 = bank()
        t = col_sums(acc[:, :], b, 0, ready, w0)
        if perm:
            t = col_sums(acc[:, :], b, 8, ready, None, perm=True)
        state["acc_used"] = t
        n = 8 if perm else 4
        s = A(small[:, 0:n], b[:, 0:2 * n:2], ACT.Sqrt, t, eps_in, state.get("small_used"), state.get("rcol_used"),
              scale=1.0 / D, bias=epsc[:, 0:1])
        bfree[i] = [s]
        r = dve(lambda e: e.reciprocal(rcol[:, 0:n], small[:, 0:n]), s, state.get("rcol_used"))
        state["small_used"] = r
        return r

    def pre_norm(g, perm=False):
        hw = []
        for k in range(KD):
            hw.append(split_h(k, X[:, k, :], c(g, k), state["x"][k]))
            sqd = add_square(X[:, k, :], k == 0, state["x"][k])
        state["x_read"] = [hw, sqd]
        return hw, sqd

    def rms_spread(sqd, perm=False):
        r = rms_cols(sqd, perm)
        i, b, w0 = bank()
        t = spread(lambda m: rcol[:, m:m + 1], r, b, w0)
        state["rcol_used"] = state["dg_used"]
        cp = A(Rb[:, :], b[:, :], ACT.Copy, t, state["Rb_used"])
        bfree[i] = [cp]
        return r, cp

    def post_norm(g, ycp):
        sqd = None
        r = rms_cols(state["acc"], False)
        i, b, w0 = bank()
        t = spread(lambda m: rcol[:, m:m + 1], r, b, w0)
        state["rcol_used"] = state["dg_used"]
        xs = []
        for k in range(KD):
            a = tt(dve, tmp[k % 2][:, :], Y[:, k, :], b[:, :], MUL, t, ycp[k], state["tmp"][k % 2])
            xs.append(stt(X[:, k, :], tmp[k % 2][:, :], g(k), X[:, k, :], MUL, ADD, a, gh_in, cst_in,
                          state.get("x_read")))
            state["tmp"][k % 2] = xs[-1]
        bfree[i] = [a]
        state["x"] = xs
        state["y_free"] = a

    def ffn_in(hw, rsp):
        aw = []
        rs = None
        for j in range(0, NF, 2):
            banks, t = gemm_group(Hh, Hl, hw)
            if rsp is not None and rs is None:
                rs = rsp()
            for i in range(2):
                g, u = bank_t[banks[i]], bank_t[banks[2 + i]]
                s = tmp[2 * i]
                v = tmp[2 * i + 1]
                jj = j + i
                if rs is not None:
                    m1 = tt(dve, s[:, :], g[:, :], Rb[:, :], MUL, t, rs, state["tmp"][2 * i])
                    s1 = A(s[:, :], s[:, :], ACT.Silu, m1)
                    s2 = tt(pool, s[:, :], s[:, :], Rb[:, :], MUL, s1)
                    gfree = m1
                else:
                    s2 = A(s[:, :], g[:, :], ACT.Silu, t, state["tmp"][2 * i])
                    gfree = s2
                m2 = tt(dve, v[:, :], u[:, :], s[:, :], MUL, t, s2, state["tmp"][2 * i + 1])
                hi = A(Ah[:, jj, :], v[:, :], ACT.Copy, m2, state["arena"])
                lo = tt(dve, Al[:, jj, :], v[:, :], f32(Ah[:, jj, :]), SUB, hi, state["arena"])
                state["tmp"][2 * i] = m2
                state["tmp"][2 * i + 1] = lo
                bfree[banks[i]] = [gfree]
                bfree[banks[2 + i]] = [m2]
                aw.append([hi, lo])
        state["h_used"] = t
        if rs is not None:
            state["Rb_used"] = [m1, s2]
        return aw

    def out_rms(nk, mh, ml, mw):
        ycp = []
        for nb in range(KD):
            i, t = gemm_row(nk, mh, ml, mw)
            cp = A(Y[:, nb, :], bank_t[i][:, :], ACT.Copy, t, state.get("y_free"), state["arena"])
            bfree[i] = [cp]
            ycp.append(cp)
            add_square(Y[:, nb, :], nb == 0, cp)
        return ycp, t

    def out_ln(nk, mh, ml, mw, half, li, last=False):
        zs = []
        zt = None
        sh = {}
        bmu = None
        for nb in range(KD):
            if nb == 6:
                pass

            def mid(k, nb=nb):
                if nb == 6 and k == nk - 1:
                    i, b, w0 = bank()
                    t = col_sums(zsum[:, :], b, 0, sh["z5"], w0)
                    cm = A(rcol[:, 16:20], b[:, 0:8:2], ACT.Copy, t, state.get("mcol_used"), scale=1.0 / 768)
                    bfree[i] = [cm]
                    sh["mcol"] = cm
                if nb == 7 and k == 3:
                    i, b, w0 = bank()
                    t = spread(lambda m: rcol[:, 16 + m:17 + m], sh["mcol"], b, w0)
                    cp = A(MUb[:, :], b[:, :], ACT.Copy, t, state["MUb_used"])
                    bfree[i] = [cp]
                    sh["mu"] = cp

            i, t = gemm_row(nk, mh, ml, mw, mid)
            z = stt(Y[:, nb, :], bank_t[i][:, :], half, X[:, nb, :], MUL, ADD, t, state["x"][nb],
                    state.get("y_free"), state["arena"])
            bfree[i] = [z]
            if nb == 1:
                zt = tt(pool, zsum[:, :], Y[:, 0, :], Y[:, 1, :], ADD, zs[0], z, state["zsum_used"])
            elif nb > 1:
                zt = tt(pool, zsum[:, :], zsum[:, :], Y[:, nb, :], ADD, zt, z, sh.get("mcol"))
            if nb == 5:
                sh["z5"] = zt
            zs.append(z)
            if nb == 6:
                z6 = zt
        gemm_end = t
        zc = []
        for k in range(KD):
            zc.append(tt(dve, Y[:, k, :], Y[:, k, :], MUb[:, :], SUB, zs[k], sh["mu"], zt))
            add_square(Y[:, k, :], k == 0, zc[k])
        state["MUb_used"] = zc[-1]
        i, b, w0 = bank()
        t = col_sums(zsum[:, :], b, 0, zt, w0)
        t = col_sums(acc[:, :], b, 8, state["acc"], None)
        state["zsum_used"] = state["acc_used"] = t
        m = A(small[:, 0:8], b[:, 0:16:2], ACT.Copy, t, state.get("small_used"), scale=1.0 / D)
        bfree[i] = [m]
        d1 = tt(dve, small[:, 8:12], small[:, 0:4], rcol[:, 16:20], SUB, m, sh["mcol"])
        d2 = tt(dve, small[:, 12:16], small[:, 8:12], small[:, 8:12], MUL, d1)
        d3 = tt(dve, small[:, 16:20], small[:, 4:8], small[:, 12:16], SUB, d2)
        s = A(small[:, 20:24], small[:, 16:20], ACT.Sqrt, d3, eps_in, bias=epsc[:, 1:2])
        r = dve(lambda e: e.reciprocal(rcol[:, 0:4], small[:, 20:24]), s, state.get("rcol_used"))
        mr = tt(dve, rcol[:, 20:24], rcol[:, 0:4], small[:, 8:12], MUL, r)
        state["small_used"] = mr
        i1, b1, w1 = bank()
        t1 = spread(lambda m: rcol[:, m:m + 1], r, b1, w1)
        i2, b2, w2 = bank()
        t2 = spread(lambda m: rcol[:, 20 + m:21 + m], mr, b2, w2)
        state["rcol_used"] = state["mcol_used"] = state["dg_used"]
        xs, hw = [], []
        for k in range(KD):
            a = tt(dve, Y[:, k, :], Y[:, k, :], b1[:, :], MUL, t1, zc[k], state["acc"])
            bb = tt(dve, Y[:, k, :], Y[:, k, :], b2[:, :], SUB, t2, a)
            x = A(X[:, k, :], Y[:, k, :], ACT.Identity, bb, zs[k], cst_in, scale=c("ln_g", li * 8 + k),
                  bias=c("ln_b", li * 8 + k))
            if last:
                sp(lambda e, k=k: e.dma_start(out_d[:, k, :], X[:, k, :]), x, sig=sem["s_out"])
                continue
            h = split_h(k, X[:, k, :], None, x)
            hw.append(h)
            xs.append(ts(pool, X[:, k, :], X[:, k, :], ALPHA, None, MUL, None, h, x))
        bfree[i1] = [a]
        bfree[i2] = [bb]
        state["y_free"] = x
        state["x"] = xs
        return hw, gemm_end

    def s5_small():
        a_re, a_im, ldt = c("a_re"), c("a_im"), c("log_dt")

        def S(i):
            return sp5[:, i, :]

        s5_in = (sem["s_s5"], 32)
        seq = [None]

        def v(fn):
            seq[0] = dve(fn, seq[0], cst_in)
            return seq[0]

        def vtt(o, a, b, op):
            return v(lambda e: e.tensor_tensor(o, a, b, op))

        def vts(o, a, s1, s2, op0, op1=None):
            if op1 is None:
                return v(lambda e: e.tensor_scalar(o, a, s1, None, op0))
            return v(lambda e: e.tensor_scalar(o, a, s1, s2, op0, op1))

        def vstt(o, a, s, b, op0, op1):
            return v(lambda e: e.scalar_tensor_tensor(o, a, s, b, op0, op1))

        t = A(S(0), ldt, ACT.Exp, cst_in)
        seq[0] = t
        vtt(S(1), S(0), a_re, MUL)
        t = vtt(S(2), S(0), a_im, MUL)
        mag = A(S(3), S(1), ACT.Exp, t)
        magic = 1.5 * 2.0 ** 23
        vts(S(4), S(2), 1.0 / (2 * math.pi), magic, MUL, ADD)
        vts(S(4), S(4), magic, None, SUB)
        c1 = 6.28125
        c2 = 0.00193500518798828125
        c3 = 2 * math.pi - c1 - c2
        vstt(S(5), S(4), -c1, S(2), MUL, ADD)
        vstt(S(5), S(4), -c2, S(5), MUL, ADD)
        vstt(S(5), S(4), -c3, S(5), MUL, ADD)
        t = vts(S(5), S(5), math.pi, -math.pi, ALU.min, ALU.max)
        sn = A(S(6), S(5), ACT.Sin, t, scale=0.5)
        cs = A(S(7), S(5), ACT.Sin, t, eps_in, scale=-0.5, bias=epsc[:, 2:3])
        seq[0] = [sn, cs, mag]
        vstt(S(8), S(6), 2.0, S(7), MUL, MUL)
        vstt(S(9), S(6), -2.0, S(6), MUL, MUL)
        vts(S(9), S(9), 1.0, None, ADD)

        def PW(i, m):
            return pw[:, i, m, :]

        v(lambda e: e.memset(PW(0, 0), 1.0))
        v(lambda e: e.memset(PW(1, 0), 0.0))
        vtt(PW(0, 1), S(3), S(9), MUL)
        vtt(PW(1, 1), S(3), S(8), MUL)
        for m in range(2, 9):
            vtt(S(10), PW(0, m - 1), PW(0, 1), MUL)
            vtt(S(11), PW(1, m - 1), PW(1, 1), MUL)
            vtt(PW(0, m), S(10), S(11), SUB)
            vtt(S(10), PW(0, m - 1), PW(1, 1), MUL)
            vtt(S(11), PW(1, m - 1), PW(0, 1), MUL)
            vtt(PW(1, m), S(10), S(11), ADD)
        vts(pw[:, 2, :, :], pw[:, 1, :, :], -1.0, None, MUL)
        for m in range(8):
            vts(PW(3, m), PW(0, 7 - m), 1.0, None, MUL)
            vts(PW(4, m), PW(1, 7 - m), 1.0, None, MUL)
        vts(M8[:, 0, 0:16], PW(0, 8), 1.0, None, MUL)
        vts(M8[:, 0, 16:32], PW(2, 8), 1.0, None, MUL)
        vts(M8[:, 1, 0:16], PW(1, 8), 1.0, None, MUL)
        vts(M8[:, 1, 16:32], PW(0, 8), 1.0, None, MUL)
        vts(S(10), PW(0, 1), -1.0, None, ADD)
        vtt(S(11), a_re, a_re, MUL)
        vtt(S(12), a_im, a_im, MUL)
        vtt(S(11), S(11), S(12), ADD)
        v(lambda e: e.reciprocal(S(12), S(11)))
        vtt(S(13), S(10), a_re, MUL)
        vtt(S(14), PW(1, 1), a_im, MUL)
        vtt(S(13), S(13), S(14), ADD)
        vtt(S(13), S(13), S(12), MUL)
        vtt(S(14), PW(1, 1), a_re, MUL)
        vtt(S(15), S(10), a_im, MUL)
        vtt(S(14), S(14), S(15), SUB)
        vtt(S(14), S(14), S(12), MUL)
        wr = S(13).unsqueeze(2).to_broadcast([P, 16, 16])
        wi = S(14).unsqueeze(2).to_broadcast([P, 16, 16])
        bre = tmp[4][:, 0:256].rearrange("p (a b) -> p a b", b=16)
        bim = tmp[4][:, 256:512].rearrange("p (a b) -> p a b", b=16)
        t3 = dgt[:, 0:2, :].rearrange("p a b -> p (a b)").rearrange("p (a b) -> p a b", b=16)
        seq[0] = [seq[0], s5_in]
        vtt(Bre[:, :, :], wr, bre, MUL)
        vtt(t3, wi, bim, MUL)
        vtt(Bre[:, :, :], Bre[:, :, :], t3, SUB)
        vtt(Bim[:, :, :], wr, bim, MUL)
        vtt(t3, wi, bre, MUL)
        t = vtt(Bim[:, :, :], Bim[:, :, :], t3, ADD)
        state["tmp"][4] = state["dg_used"] = t
        return t

    def s5_big(small_in):
        af = [state["arena"], small_in]

        def powers(i, n):
            return pw[:, i, 0:n, :].rearrange("p m a -> p a m").unsqueeze(3).to_broadcast([P, 16, n, 16])

        def chans(ap, n):
            return ap.unsqueeze(2).to_broadcast([P, 16, n, 16])

        seq = [af]

        def p(o, a, b, op):
            for pr in range(0, 16, 4):
                last = pool(lambda e, pr=pr: e.tensor_tensor(o[:, pr:pr + 4], a[:, pr:pr + 4], b[:, pr:pr + 4], op),
                            *seq)
            seq[0] = last
            return last

        wre, wim = Wri[:, 0], Wri[:, 1]
        rr, ri = powers(3, 8), powers(4, 8)
        br, bi = chans(Bre[:, :, :], 8), chans(Bim[:, :, :], 8)
        p(wre, rr, br, MUL)
        p(Wt[:, :, :, :], ri, bi, MUL)
        p(wre, wre, Wt[:, :, :, :], SUB)
        p(wim, rr, bi, MUL)
        p(Wt[:, :, :, :], ri, br, MUL)
        w_in = p(wim, wim, Wt[:, :, :, :], ADD)
        return w_in

    def s5_big2(w1_read):
        def powers(i, n):
            return pw[:, i, 0:n, :].rearrange("p m a -> p a m").unsqueeze(3).to_broadcast([P, 16, n, 16])

        seq = [[w1_read, state["arena"]]]

        def p(o, a, b, op):
            for pr in range(0, 16, 4):
                last = pool(lambda e, pr=pr: e.tensor_tensor(o[:, pr:pr + 4], a[:, pr:pr + 4], b[:, pr:pr + 4], op),
                            *seq)
            seq[0] = last
            return last

        cr = MUb[:, 0:256].rearrange("p (a b) -> p a b", b=16).unsqueeze(2).to_broadcast([P, 16, 9, 16])
        ci = MUb[:, 256:512].rearrange("p (a b) -> p a b", b=16).unsqueeze(2).to_broadcast([P, 16, 9, 16])
        gr, gi, gt = Gre[:, :, :, :], Gim[:, :, :, :], Gt[:, :, :, :]
        p(gr, powers(0, 9), cr, MUL)
        p(gt, powers(1, 9), ci, MUL)
        p(gr, gr, gt, SUB)
        p(gi, powers(2, 9), cr, MUL)
        p(gt, powers(0, 9), ci, MUL)
        return p(gi, gi, gt, SUB)

    def mixer_1(s5_in):
        hw, sqd = pre_norm("g_mpre", perm=True)
        w_in = s5_big(s5_in)
        banks, t = gemm_tokens(lambda h, k, m: h[:, k, m::4], hw)
        rc, rb = rms_spread(sqd, perm=True)
        u2 = []
        for m in range(4):
            b = bank_t[banks[m]]
            e = A(U2[:, :, m, :], b[:, :].rearrange("p (g n) -> p g n", n=16), ACT.Copy, t, rc, state["arena"],
                  scale=rcol[:, 4 + m:5 + m])
            bfree[banks[m]] = [e]
            u2.append(e)
        banks, t = gemm_group(Hh, Hl, hw)
        qk = []
        for i in range(4):
            e = stt(Qf[:, i, :], bank_t[banks[i]][:, :], 0.125, Rb[:, :], MUL, MUL, t, rb, state["arena"])
            bfree[banks[i]] = [e]
            qk.append(e)
        ups = []
        for q in range(8):
            i, b, w0 = bank()
            for s in range(4):
                t = tr(b[0:64, s * P:(s + 1) * P], U2[:, 4 * q + s, :, :], ident, u2, w0, cst_in, sig=s == 3)
            src = b[0:64, :].rearrange("p (g j s) -> p g j s", g=4, s=2)
            e1 = A(Up[0:64, 4 * q:4 * q + 4, :], src[:, :, :, 0], ACT.Copy, t, state["arena"])
            e2 = A(Up[64:128, 4 * q:4 * q + 4, :], src[:, :, :, 1], ACT.Copy, t, state["arena"])
            bfree[i] = [e2]
            ups.append(e2)
        u2_read = t
        banks, t = gemm_group(Hh, Hl, hw)
        for i in range(4):
            e = tt(dve, Kf[:, i, :], bank_t[banks[i]][:, :], Rb[:, :], MUL, t, rb, state["arena"])
            bfree[banks[i]] = [e]
            qk.append(e)
        state["Rb_used"] = e
        w1 = []
        for q in range(8):
            i, b, w0 = bank()
            for s in range(4):
                t = tr(b[:, s * P:(s + 1) * P], Wri[:, s % 2, 2 * q + s // 2, :, :], ident, w_in, w0, cst_in,
                       sig=s == 3)
            for s in range(2):
                src = b[:, s * 256:(s + 1) * 256].rearrange("p (r g q) -> p g r q", r=2, g=2)
                if q % 2:
                    e = A(W1[:, 2 * q + s, :, :, :], src, ACT.Copy, t, state["arena"])
                else:
                    e = dve(lambda en, q=q, s=s, src=src: en.tensor_copy(W1[:, 2 * q + s, :, :, :], src), t,
                            state["arena"])
                w1.append(e)
            bfree[i] = w1[-2:]
        w1_read = t
        g_in = s5_big2(w1_read)
        banks, t = gemm_tokens(lambda h, k, m: h[:, k, m * P:(m + 1) * P], hw)
        state["h_used"] = t
        vt = []
        for m in range(4):
            e = A(Vt[:, m, :], bank_t[banks[m]][:, :], ACT.Copy, t, rc, state["arena"], scale=rcol[:, m:m + 1])
            bfree[banks[m]] = [e]
            vt.append(e)
        state["rcol_used"] = [state["rcol_used"], e, u2]
        w3z = pool(lambda e: e.memset(W3[:, :, :], 0.0), u2_read)
        x0 = pool(lambda e: e.memset(XS[:, 0, :, :], 0.0), w1_read, g_in)
        fs = []
        for q in range(4):
            i, b, w0 = bank()
            for g8 in range(8):
                g = 8 * q + g8
                t = mm(b[:, g8 * 64:(g8 + 1) * 64], W1[:, g // 2, g % 2, :, :], Up[:, g, :], True, True, w1, ups, w0,
                       sig=g8 == 7, skip=True)
            v4 = b[:, :].rearrange("p (a g j) -> p a g j", a=4, g=2)
            ev = []
            for g2 in range(2):
                for ri in range(2):
                    dst = FS[64 * g2:64 * g2 + 64, :, ri, 4 * q:4 * q + 4].rearrange("p j a -> p a j")
                    src = v4[64 * ri:64 * ri + 64, :, g2, :]
                    if ri == 0:
                        ev.append(A(dst, src, ACT.Copy, t, g_in))
                    else:
                        ev.append(dve(lambda en, dst=dst, src=src: en.tensor_copy(dst, src), t, g_in))
            bfree[i] = ev
            fs += ev
        f_read = t
        kr = []
        for q in range(8):
            i, b, w0 = bank()
            par = q % 2
            r = slice(64 * par, 64 * par + 64)
            for s in range(4):
                o = b[0:16, s * P:(s + 1) * P]
                pr = 4 * (q // 2) + s
                mm(o, Bre[r, pr, :], Gre[r, pr, 0:8, :], True, False, g_in, w0, f_read, skip=True)
                t = mm(o, Bim[r, pr, :], Gim[r, pr, 0:8, :], False, True, sig=s == 3, skip=True)
            e = A(Kr[0:16, 8 * (q // 2) + par:8 * (q // 2) + 8:2, :], b[0:16, :].rearrange("p (s n) -> p s n", s=4),
                  ACT.Copy, t, f_read)
            bfree[i] = [e]
            kr.append(e)
        dsk = tmp[4][0:16, :].rearrange("p (g n) -> p g n", n=16)
        e = tt(dve, dsk, ident[0:16, 0:16].unsqueeze(1).to_broadcast([16, 32, 16]),
               c("d_skip")[0:16, :].unsqueeze(2).to_broadcast([16, 32, 16]), MUL, state["tmp"][4], cst_in)
        e = tt(dve, Kr[0:16, :, 0:16], Kr[0:16, :, 0:16], dsk, ADD, e, kr)
        state["tmp"][4] = e
        for m in range(8):
            sp(lambda en, m=m: en.dma_start(W3[16 * m:16 * m + 16, :, 16 * m:P], Kr[0:16, :, 0:P - 16 * m]), e, w3z,
               sig=sem["s_w3"])
        w3_in = (sem["s_w3"], 16 * 8)
        sp(lambda en: en.dma_start(Dp[:, :], att_d[:, 0, :]), state["zsum_used"], sig=sem["s_att"])
        sp(lambda en: en.dma_start(Cn[:, :], att_d[:, 1, :]), g_in, sig=sem["s_att"])
        att_in = (sem["s_att"], 32)
        xw = x0
        M = M8[:, :, :]
        st = small[:, 0:64].rearrange("p (a b) -> p a b", a=2)
        sx = state.get("small_used")
        for j in range(63):
            xj = XS[:, j, :, :].rearrange("p a b -> p (a b)").unsqueeze(1).to_broadcast([P, 2, 32])
            a = pool(lambda e, xj=xj: e.tensor_tensor(st, xj, M, MUL), xw, fs, s5_in, sx)
            b_ = pool(lambda e, j=j: e.tensor_tensor(XS[:, j + 1, :, :], st[:, :, 0:16], FS[:, j, :, :], ADD), a)
            xw = pool(lambda e, j=j: e.tensor_tensor(XS[:, j + 1, :, :], XS[:, j + 1, :, :], st[:, :, 16:32], ADD), b_)
        state["small_used"] = xw

        def s5_out():
            y2 = []
            for q in range(8):
                i, b, w0 = bank()
                par = q % 2
                r = slice(64 * par, 64 * par + 64)
                for s in range(4):
                    pr = 4 * (q // 2) + s
                    g = 2 * pr + par
                    o = b[0:64, s * P:(s + 1) * P]
                    mm(o, Up[:, g, :], W3[:, g, :], True, False, w3_in, xw, w0, skip=True)
                    mm(o, XS[r, :, 0, pr], Gre[r, pr, 1:9, :], False, False, skip=True)
                    t = mm(o, XS[r, :, 1, pr], Gim[r, pr, 1:9, :], False, True, sig=s == 3, skip=True)
                src = b[0:64, :].rearrange("p (s t n) -> p s t n", s=4, t=8)
                g0 = 8 * (q // 2) + par
                dst = Y2[0:64, :, :].rearrange("p t (g n) -> p g t n", n=16)[:, g0:g0 + 7:2, :, :]
                if q % 2:
                    e = A(dst, src, ACT.Copy, t, w3_in)
                else:
                    e = dve(lambda en, dst=dst, src=src: en.tensor_copy(dst, src), t, w3_in)
                bfree[i] = [e]
                y2.append(e)
            mats_read = t
            yw = []
            for cb in range(4):
                i, b, w0 = bank()
                for tt_ in range(8):
                    t = tr(b[:, tt_ * 64:(tt_ + 1) * 64], Y2[0:64, tt_, P * cb:P * (cb + 1)], ident[0:64, 0:64], y2, w0,
                           sig=tt_ == 7)
                g = A(yg[:, cb, :].rearrange("p (j t) -> p t j", t=8), b[:, :].rearrange("p (t j) -> p t j", t=8),
                      ACT.Gelu_apprx_tanh, t, mats_read)
                bfree[i] = [g]
                hi = A(yh[:, cb, :], yg[:, cb, :], ACT.Copy, g, mats_read)
                lo = tt(dve, yl[:, cb, :], yg[:, cb, :], f32(yh[:, cb, :]), SUB, hi, mats_read)
                yw.append([hi, lo])
            return yw

        def head(h):
            hb, off = h // 2, 64 * (h % 2)
            slope = 2.0 ** (-(h + 1))
            r = slice(off, off + 64)
            ptw = []
            for tb in range(4):
                n = P * (tb + 1)
                i, b, w0 = bank()
                t = mm(b[:, 0:n], Qf[r, hb, tb * P:(tb + 1) * P], Kf[r, hb, 0:n], True, True, qk, w0, sig=True)
                s, p_ = tmp[tb % 2], tmp[2 + tb % 2]
                o = 32 + 4 * (tb % 2)
                s1 = stt(s[:, 0:n], Dp[:, T - n:T], -slope, b[:, 0:n], MUL, ADD, t, att_in, state["tmp"][tb % 2])
                bfree[i] = [s1]
                mx = dve(lambda e, o=o, s=s, n=n: e.tensor_reduce(rcol[:, o:o + 1], s[:, 0:n], AX_X, ALU.max,
                                                                 negate=True), s1, state["tmp"][2 + tb % 2])
                ex = A(s[:, 0:n], s[:, 0:n], ACT.Exp, mx, bias=rcol[:, o:o + 1])
                pc = stt(p_[:, 0:n], s[:, 0:n], 1.0, Cn[:, T - n:T], MUL, MUL, ex, state["tmp"][2 + tb % 2],
                         accum_out=rcol[:, o + 1:o + 2])
                state["tmp"][tb % 2] = pc
                rd = dve(lambda e, o=o: e.reciprocal(rcol[:, o + 2:o + 3], rcol[:, o + 1:o + 2]), pc)
                sc = A(p_[:, 0:n], p_[:, 0:n], ACT.Copy, rd, scale=rcol[:, o + 2:o + 3])
                i, b, w0 = bank()
                for sb in range(tb + 1):
                    t = tr(b[:, sb * P:(sb + 1) * P], p_[:, sb * P:(sb + 1) * P], ident, sc, w0, sig=sb == tb)
                state["tmp"][2 + tb % 2] = t
                e = dve(lambda en, b=b, tb=tb, n=n: en.tensor_copy(
                    PT[:, 0:tb + 1, tb * P:(tb + 1) * P], b[:, 0:n].rearrange("p (s t) -> p s t", t=P)),
                    t, state.get("pt_used"), w_in, state["arena"])
                bfree[i] = [e]
                ptw.append(e)
            if h % 2 == 0:
                state["ob"] = bank()
            i, b, w0 = state["ob"]
            for sb in range(4):
                t = mm(b[r, sb * P:T], Vt[:, sb, 64 * h:64 * h + 64], PT[:, sb, sb * P:T], sb == 0, sb == 3, vt, ptw, w0,
                       sig=sb == 3)
            state["pt_used"] = t
            if h % 2 == 0:
                return None
            hi = A(Hh[:, hb, :], b[:, :], ACT.Copy, t, state["h_used"])
            lo = tt(dve, Hl[:, hb, :], b[:, :], f32(Hh[:, hb, :]), SUB, hi, state["h_used"])
            bfree[i] = [hi, lo]
            return [hi, lo]

        mw = []
        for h in range(HEADS):
            m = head(h)
            if m:
                mw.append(m)
            if h == 5:
                yw = s5_out()
        for nb in range(4):
            i, t = gemm_row(4, yh, yl, yw)
            s = A(tmp[nb][:, :], bank_t[i][:, :], ACT.Sigmoid, t, state["tmp"][nb], cst_in, bias=c("b_glu", nb))
            bfree[i] = [s]
            m = tt(dve, tmp[nb][:, :], tmp[nb][:, :], yg[:, nb, :], MUL, s)
            hi = A(Hh[:, 4 + nb, :], tmp[nb][:, :], ACT.Copy, m, state["h_used"])
            lo = tt(dve, Hl[:, 4 + nb, :], tmp[nb][:, :], f32(Hh[:, 4 + nb, :]), SUB, hi, state["h_used"])
            state["tmp"][nb] = lo
            mw.append([hi, lo])
        state["zsum_used"] = state["MUb_used"] = lo
        state["arena"] = [t, lo]
        state["y_free"] = None
        ycp, t = out_rms(KD, Hh, Hl, mw)
        state["h_used"] = t
        post_norm(lambda k: c("g_mpost", k), ycp)

    def mixer_2(l, hw):
        af = state["arena"]
        lbc = hcol[:, 0:8]
        zs = pool(lambda e: e.memset(Sc[:, :, :, :], 0.0), af)
        zp = pool(lambda e: e.memset(U3[:, :, 0:16], 0.0), af)
        zp = pool(lambda e: e.memset(PA[:, :, 0:16], 0.0), af)
        banks, t = gemm_group(Hh, Hl, hw)
        ft, ks = [], []
        for h in range(4):
            b = bank_t[banks[h]]
            s = A(FT[:, h, :], b[:, :], ACT.Sigmoid, t, af)
            s2 = A(KS[:, h, :], b[:, :], ACT.Sigmoid, t, af, scale=-1.0)
            bfree[banks[h]] = [s2]
            ft.append(ts(dve, FT[:, h, :], FT[:, h, :], hcol[:, 8 + 4 * l + h:9 + 4 * l + h],
                         hcol[:, 4 * l + h:4 * l + h + 1], MUL, ADD, s, lb_in))
            ks.append(ts(dve, KS[:, h, :], KS[:, h, :], hcol[:, 8 + 4 * l + h:9 + 4 * l + h], None, MUL, None, s2, lb_in))
        banks, t = gemm_group(Hh, Hl, hw)
        qp = []
        for h in range(4):
            e = A(QP[:, h, :], bank_t[banks[h]][:, :], ACT.Copy, t, af, scale=P ** -0.5)
            bfree[banks[h]] = [e]
            qp.append(e)

        flat4 = QP[:, :, :].rearrange("p h t -> p (h t)")
        kflat = KS[:, :, :].rearrange("p h t -> p (h t)")
        fflat = FT[:, :, :].rearrange("p h t -> p (h t)")
        cur = {"q": qp, "k": ks, "t": [ft], "T": fflat, "toff": 0, "used": None, "sw": []}

        def decays(n):
            if n == 0:
                return
            if n == 1:
                cur["q"] = [tt(dve, flat4, flat4, fflat, MUL, cur["q"], ft, cur["used"])]
                return
            m = n // 2
            nb = 4 * T // n
            Tm = cur["T"].rearrange("p (b s) -> p b s", s=2)
            q4 = flat4.rearrange("p (b s i) -> p b s i", s=2, i=m)
            k4 = kflat.rearrange("p (b s i) -> p b s i", s=2, i=m)
            left = Tm[:, :, 0:1].to_broadcast([P, nb, m])
            right = Tm[:, :, 1:2].to_broadcast([P, nb, m])
            q = tt(dve, q4[:, :, 1, :], q4[:, :, 1, :], left, MUL, cur["q"], cur["t"], cur["used"])
            k = tt(pool, k4[:, :, 0, :], k4[:, :, 0, :], right, MUL, cur["k"], cur["t"], cur["used"])
            o = cur["toff"]
            tn = TT[:, o:o + nb]
            t_ = tt(pool, tn, Tm[:, :, 0], Tm[:, :, 1], MUL, cur["t"], af)
            cur.update(q=[q], k=[k], t=[t_], T=tn, toff=o + nb)

        def level(li):
            decays(LEVELS[li])
            sw = []
            for h in range(4):
                i, b, w0 = bank()
                for m in range(4):
                    s = slice(m * P, (m + 1) * P)
                    t = mm(b[:, s], KS[:, h, s], QP[:, h, s], True, True, cur["q"], cur["k"], w0, sig=m == 3, skip=True)
                dst = Sc[:, h, :, :].rearrange("p i t -> p (i t)")
                view = bass.AP(tensor=dst.tensor, offset=dst.offset, ap=[list(dst.ap[0]), [640, 4], [1, P]])
                mk = msk[:, li, :].unsqueeze(1).to_broadcast([P, 4, P])
                src = b[:, :].rearrange("p (i t) -> p i t", i=4)
                e = dve(lambda en, view=view, mk=mk, src=src: en.copy_predicated(view, mk, src), t, zs, msk_in,
                        cur["sw"][h] if cur["sw"] else None)
                bfree[i] = [e]
                sw.append(e)
            cur["used"] = t
            cur["sw"] = sw

        def far(n):
            decays(n)
            for h in range(4):
                i, b, w0 = bank()
                if n == P:
                    for a in range(2):
                        s, d = slice(2 * a * P, (2 * a + 1) * P), slice((2 * a + 1) * P, (2 * a + 2) * P)
                        t = mm(b[:, a * P:(a + 1) * P], KS[:, h, s], QP[:, h, d], True, True, cur["q"], cur["k"], w0,
                               sig=a == 1, skip=True)
                    e1 = A(Sc[:, h, 0, P:2 * P], b[:, 0:P], ACT.Copy, t, zs)
                    e2 = A(Sc[:, h, 2, 3 * P:4 * P], b[:, P:2 * P], ACT.Copy, t, zs)
                    cur.setdefault("far", []).extend([e1, e2])
                else:
                    for a in range(2):
                        t = mm(b[:, a * 256:(a + 1) * 256], KS[:, h, a * P:(a + 1) * P], QP[:, h, 256:512], True, True,
                               cur["q"], cur["k"], w0, sig=a == 1, skip=True)
                    e2 = A(Sc[:, h, 0:2, 256:512], b[:, :].rearrange("p (a t) -> p a t", a=2), ACT.Copy, t, zs)
                    cur["far"].append(e2)
                bfree[i] = [e2]
            cur["used"] = t

        level(0)
        banks, t = gemm_tokens(lambda h, k, m: h[:, k, m * P:(m + 1) * P], hw)
        vt = []
        for m in range(4):
            e = A(V2[:, m, :], bank_t[banks[m]][:, :], ACT.Copy, t, af)
            bfree[banks[m]] = [e]
            vt.append(e)
        level(1)
        level(2)
        banks, t = gemm_group(Hh, Hl, hw)
        ug = []
        for g in range(4):
            e = A(U3[:, g, 16:16 + T], bank_t[banks[g]][:, :], ACT.Copy, t, af, zp)
            bfree[banks[g]] = [e]
            ug.append(e)
        level(3)
        level(4)
        banks, t = gemm_group(Hh, Hl, hw)
        h_used = t
        sg = []
        for h in range(4):
            e = A(Sg[:, h, :], bank_t[banks[h]][:, :], ACT.Silu, t, af)
            bfree[banks[h]] = [e]
            sg.append(e)
        state["h_used"] = h_used
        mw = [None] * KD
        pw_ = []
        pa = None
        for g in range(4):
            w = 2 << g
            src, sw_ = U3[:, g, :], ug[g]
            d = 1
            n = 0
            while d < w:
                dst = PA[:, n % 2, :]
                sw_ = tt(pool, dst[:, 16:16 + T], src[:, 16:16 + T], src[:, 16 - d:16 - d + T], ADD, sw_, zp, pa)
                src = dst
                d *= 2
                n += 1
            last = src
            p_ = tmp[g]
            e1 = stt(p_[:, :], last[:, 16:16 + T], 1.0 / w, U3[:, g, 16:16 + T], MUL, SUB, sw_, state["tmp"][g])
            e2 = tt(dve, tmp[4][:, 0:16], last[:, 16:32], c("rcount", 16 * g, 16), MUL, sw_, cst_in, state["tmp"][4])
            e3 = tt(dve, p_[:, 0:16], tmp[4][:, 0:16], U3[:, g, 16:32], SUB, e2, e1)
            pa = e2
            state["tmp"][4] = e3
            hi = A(Hh[:, g, :], p_[:, :], ACT.Copy, e3, h_used)
            lo = tt(dve, Hl[:, g, :], p_[:, :], f32(Hh[:, g, :]), SUB, hi, h_used)
            state["tmp"][g] = lo
            pw_.append([hi, lo])
        level(5)
        level(6)
        for g in range(4):
            i, b, w0 = bank()
            hi, lo, w, unit = wtile()
            t = mm3(b[:, :], hi, lo, Hh[:, g, :], Hl[:, g, :], True, True, [w, pw_[g], w0], unit, sig=True)
            sc = c("pool_scale", 4 * l + g)
            hi = A(Hh[:, g, :], b[:, :], ACT.Copy, t, scale=sc)
            lo = stt(Hl[:, g, :], b[:, :], sc, f32(Hh[:, g, :]), MUL, SUB, hi)
            bfree[i] = [hi, lo]
            mw[g] = [hi, lo]
        level(7)
        far(128)
        far(256)
        oh = []
        i0, b0, wb = bank()
        for h in range(4):
            i, b, w0 = bank()
            for m in range(4):
                t = mm(b[:, m * P:T], V2[:, m, h * P:(h + 1) * P], Sc[:, h, m, m * P:T], m == 0, m == 3, vt, cur["sw"],
                       cur["far"], w0, sig=m == 3)
            e = A(Oh[:, h, :], b[:, :], ACT.Copy, t, af)
            s = A(tmp[h][:, :], b[:, :], ACT.Square, t, state["tmp"][h])
            bfree[i] = [s]
            t = col_sums(tmp[h][:, :], b0, 8 * h, s, wb)
            state["tmp"][h] = t
            oh.append(e)
        s = A(small[:, 0:16], b0[:, 0:32:2], ACT.Sqrt, t, eps_in, state.get("small_used"), scale=1.0 / P,
              bias=epsc[:, 0:1])
        bfree[i0] = [s]
        r = dve(lambda e: e.reciprocal(rcol[:, 0:16], small[:, 0:16]), s, state.get("rcol_used"))
        state["small_used"] = r
        for h in range(4):
            i, b, w0 = bank()
            t = spread(lambda m: rcol[:, 4 * h + m:4 * h + m + 1], r, b, w0)
            state["rcol_used"] = t
            e = tt(dve, Oh[:, h, :], Oh[:, h, :], b[:, :], MUL, t, oh[h])
            bfree[i] = [e]
            e = stt(tmp[h][:, :], Oh[:, h, :], c("hg", l), Sg[:, h, :], MUL, MUL, e, sg[h], state["tmp"][h], cst_in)
            hi = A(Hh[:, 4 + h, :], tmp[h][:, :], ACT.Copy, e, h_used)
            lo = tt(dve, Hl[:, 4 + h, :], tmp[h][:, :], f32(Hh[:, 4 + h, :]), SUB, hi, h_used)
            state["tmp"][h] = lo
            mw[4 + h] = [hi, lo]
        state["arena"] = [lo, t]
        state["y_free"] = None
        hw, t = out_ln(KD, Hh, Hl, mw, 1.0, 3 * l + 1)
        return hw

    def ffn_1(pre, post_g):
        hw, sqd = pre_norm(pre)
        aw = ffn_in(hw, lambda: rms_spread(sqd)[1])
        state["arena"] = None
        ycp, t = out_rms(NF, Ah, Al, aw)
        state["arena"] = t
        post_norm(post_g, ycp)
        state["arena"] = [t, state["x"][-1]]

    def ffn_2(hw, li, last=False):
        aw = ffn_in(hw, None)
        state["arena"] = None
        hw, t = out_ln(NF, Ah, Al, aw, 0.5, li, last)
        state["arena"] = [t, state["y_free"]]
        return hw

    s5_in = s5_small()
    lb = c("lb")
    d = tt(dve, hcol[:, 16:20], lb[:, 0:4], lb[:, 4:8], ALU.max, cst_in)
    d = tt(dve, hcol[:, 20:24], lb[:, 0:4], hcol[:, 16:20], SUB, d)
    d = tt(dve, hcol[:, 24:28], lb[:, 4:8], hcol[:, 16:20], SUB, d)
    e = A(hcol[:, 20:28], hcol[:, 20:28], ACT.Exp, d)
    d = tt(dve, hcol[:, 16:20], hcol[:, 20:24], hcol[:, 24:28], ADD, e)
    d = dve(lambda e: e.reciprocal(hcol[:, 28:32], hcol[:, 16:20]), d)
    d = tt(dve, hcol[:, 20:24], hcol[:, 20:24], hcol[:, 28:32], MUL, d)
    d = tt(dve, hcol[:, 24:28], hcol[:, 24:28], hcol[:, 28:32], MUL, d)
    d = tt(dve, hcol[:, 24:28], hcol[:, 20:24], hcol[:, 24:28], ADD, d)
    d = tt(dve, hcol[:, 0:4], hcol[:, 20:24], hcol[:, 20:24], SUB, d)
    d = tt(dve, hcol[:, 4:8], hcol[:, 24:28], hcol[:, 20:24], SUB, d)
    lb_in = ts(dve, hcol[:, 8:16], hcol[:, 0:8], -1.0, 1.0, MUL, ADD, d)

    ffn_1("g_f1pre", lambda k: gh[:, k:k + 1])
    mixer_1(s5_in)
    ffn_1("g_f2pre", lambda k: gh[:, 8 + k:9 + k])
    hw = []
    xs = []
    for k in range(KD):
        hw.append(split_h(k, X[:, k, :], None, state["x"][k]))
        xs.append(ts(pool, X[:, k, :], X[:, k, :], ALPHA, None, MUL, None, hw[k]))
    state["x"] = xs
    for l in range(2):
        hw = ffn_2(hw, 3 * l)
        hw = mixer_2(l, hw)
        hw = ffn_2(hw, 3 * l + 2, last=l == 1)
    assert pos[0] == n_units * 8, (pos[0], n_units)
    sp(lambda e: e.wait_ge(sem["s_out"], 16 * KD), sig=False)

    with nc.Block() as block:
        @block.sync
        def _(eng):
            run_queue(eng, sp)

        @block.tensor
        def _(eng):
            run_queue(eng, pe)

        @block.scalar
        def _(eng):
            run_queue(eng, act)

        @block.vector
        def _(eng):
            run_queue(eng, dve)

        @block.gpsimd
        def _(eng):
            run_queue(eng, pool)


def attention_tables():
    import numpy as np

    t = np.arange(P)[:, None]
    s = np.arange(T)[None, :] - 3 * P
    dist = t - s
    count = np.zeros(dist.shape, np.float32)
    for window, dilation in ((128, 1), (512, 4), (2048, 16)):
        count += (dist >= 0) & (dist <= window) & (dist % dilation == 0)
    far = np.where(count > 0, dist, 1e30).astype(np.float32)
    return np.stack([far, count], 1)


def level_masks():
    import numpy as np

    s, t = np.arange(P)[:, None], np.arange(P)[None, :]
    masks = [s == t]
    for n in LEVELS[1:]:
        masks.append((s // (2 * n) == t // (2 * n)) & (s // n % 2 == 0) & (t // n % 2 == 1))
    return np.stack(masks, 1).astype(np.float32).reshape(P, 2, 512)


def kernel(**inputs):
    import numpy as np
    import concourse.bacc as bacc
    from concourse.bass_utils import run_bass_kernel_spmd

    a = {k: np.asarray(v) for k, v in inputs.items()}

    def tiles(w):
        k, n = w.shape
        return w.reshape(k // P, P, n // P, P).transpose(0, 2, 1, 3)

    mats = {"f1_in": tiles(a["ffn1_w_in"][0]), "f1_out": tiles(a["ffn1_w_out"][0]), "mix_in": tiles(a["w_mix_in"][0]),
            "glu": tiles(a["w_glu"][0]), "mix_out": tiles(a["w_mix_out"][0]), "f2_in": tiles(a["ffn2_w_in"][0]),
            "f2_out": tiles(a["ffn2_w_out"][0])}
    for l in range(2):
        for n in (1, 2):
            mats[f"gate{n}_{l}"] = tiles(a[f"ffn{n}_gate_2"][l])
            mats[f"up{n}_{l}"] = tiles(a[f"ffn{n}_up_2"][l])
            mats[f"down{n}_{l}"] = tiles(a[f"ffn{n}_down_2"][l])
        mats[f"in_{l}"] = tiles(a["w_in_2"][l])
        mats[f"out_{l}"] = tiles(a["w_out_2"][l])
        for g in range(4):
            mats[f"pool{g}_{l}"] = tiles(a["pool_w_2"][l, g])
    plan = stream_plan()
    assert len(plan) % 8 == 0
    stream = np.empty((len(plan) // 8, P, 8, P), np.float32)
    for i, (name, k, n) in enumerate(plan):
        stream[i // 8, :, i % 8, :] = mats[name][k, n]
    stream = stream.reshape(len(plan) // 8, P, 8 * P)

    def cols(v, n):
        return v.reshape(n, P).T

    def pairs(v):
        v = v.reshape((16, 2, 64) + v.shape[2:])
        return np.moveaxis(v, 0, 2).reshape((P, 16) + v.shape[3:])

    cst = np.zeros((P, NCOLS), np.float32)

    def put(name, v):
        cst[:v.shape[0], COLS[name][0]:COLS[name][1]] = v

    put("ident", np.eye(P, dtype=np.float32))
    for name, key in (("g_f1pre", "ffn1_pre_g"), ("g_f1post", "ffn1_post_g"), ("g_mpre", "mix_pre_g"),
                      ("g_mpost", "mix_post_g"), ("g_f2pre", "ffn2_pre_g"), ("g_f2post", "ffn2_post_g")):
        put(name, cols(a[key], 8))
    put("ln_g", cols(a["ln_g_2"], 48))
    put("ln_b", cols(a["ln_b_2"], 48))
    put("pool_scale", cols(a["pool_scale_2"], 8))
    put("lb", cols(a["lb_param_2"], 8))
    put("hg", cols(a["hgrn_norm_g_2"], 2))
    put("b_glu", cols(a["b_glu"], 4))
    put("a_re", pairs(a["a_re"][0]))
    put("a_im", pairs(a["a_im"][0]))
    put("log_dt", pairs(np.broadcast_to(a["log_dt"][0][:, None], (32, 64))))
    put("d_skip", a["d_skip"].reshape(32, 16).T)
    pos = np.arange(16)
    put("rcount", np.broadcast_to(np.concatenate(
        [1.0 / np.minimum(pos + 1, w) for w in (2, 4, 8, 16)]).astype(np.float32), (P, 64)))
    s5 = np.concatenate([pairs(a["b_re"][0]).reshape(P, 256), pairs(a["b_im"][0]).reshape(P, 256),
                         pairs(a["c_re"][0].transpose(0, 2, 1)).reshape(P, 256),
                         pairs(a["c_im"][0].transpose(0, 2, 1)).reshape(P, 256)], 1).reshape(P, 2, 512)
    x = a["x"][0].T.reshape(KD, P, T).transpose(1, 0, 2)
    arrays = {"x_t": x, "weights": stream, "vectors": cst, "ssm": s5, "attention": attention_tables(),
              "masks": level_masks()}
    arrays = {k: np.ascontiguousarray(v) for k, v in arrays.items()}

    nc = bacc.Bacc("TRN2", target_bir_lowering=False, num_devices=1, dynamic_dma_scratch_size=1024)
    args = [nc.dram_tensor(k, v.shape, mybir.dt.from_np(v.dtype), kind="ExternalInput").ap() for k, v in arrays.items()]
    out = nc.dram_tensor("y_t", (P, KD, T), F32, kind="ExternalOutput").ap()
    build(nc, *args, out)
    r = run_bass_kernel_spmd(nc, [arrays], core_ids=[0])
    y = np.asarray(r.results[0]["y_t"])
    return y.transpose(1, 0, 2).reshape(D, T).T[None].copy()
```

```python
import math

import concourse.bass as bass
from concourse import mybir

P = 128
T = 512
D = 1024
KD = D // P
NF = 2816 // P
F32 = mybir.dt.float32
F32R = mybir.dt.float32r
U8 = mybir.dt.uint8
ALU = mybir.AluOpType
ACT = mybir.ActivationFunctionType
AX_X = mybir.AxisListType.X
MUL, ADD, SUB = ALU.mult, ALU.add, ALU.subtract

ALPHA = 4.0 ** 0.25
NR = 3
NH = 3
AHEAD = 2
EARLY = 2
HEADS = 8
LEVELS = (0, 1, 2, 4, 8, 16, 32, 64)

COLS = {}
_at = 0
for _name, _n in (("ident", 128), ("g_f1pre", 8), ("g_f1post", 8), ("g_mpre", 8), ("g_mpost", 8),
                  ("g_f2pre", 8), ("g_f2post", 8), ("ln_g", 48), ("ln_b", 48), ("pool_scale", 8),
                  ("lb", 8), ("hg", 2), ("b_glu", 4), ("a_re", 16), ("a_im", 16), ("log_dt", 16),
                  ("d_skip", 32), ("rcount", 64)):
    COLS[_name] = (_at, _at + _n)
    _at += _n
NCOLS = _at


def stream_plan():
    plan = []

    def groups(name, cols):
        for k in range(KD):
            plan.extend((n, k, c) for n, c in zip(name, cols))

    def halves(name, between=lambda: None):
        plan.extend((name, k, c) for c in range(4) for k in range(4))
        between()
        plan.extend((name, 4 + k, c) for c in range(4) for k in range(4))
        plan.extend((name, k, c) for c in range(4, KD) for k in range(KD))

    def rows(name, nk, nn):
        plan.extend((name, k, c) for c in range(nn) for k in range(nk))

    def ffn_in(gate, up, base):
        for j in range(0, NF, 2):
            groups((gate, gate, up, up), (j, j + 1, base + j, base + j + 1))

    ffn_in("f1_in", "f1_in", NF)
    rows("f1_out", NF, KD)
    for cols in ((12, 13, 14, 15), (8, 9, 10, 11), (0, 1, 4, 5), (2, 3, 6, 7)):
        groups(("mix_in",) * 4, cols)
    halves("mix_out", lambda: rows("glu", 4, 4))
    ffn_in("f2_in", "f2_in", NF)
    rows("f2_out", NF, KD)
    for l in range(2):
        ffn_in(f"gate1_{l}", f"up1_{l}", 0)
        rows(f"down1_{l}", NF, KD)
        for c in (8, 4, 12, 0, 16):
            groups((f"in_{l}",) * 4, range(c, c + 4))
        plan.extend((f"pool{g}_{l}", 0, 0) for g in range(4))
        halves(f"out_{l}")
        ffn_in(f"gate2_{l}", f"up2_{l}", 0)
        rows(f"down2_{l}", NF, KD)
    return plan


class Queue:

    def __init__(self, sem):
        self.sem = sem
        self.ops = []
        self.n = 0

    def __call__(self, fn, *waits, sig=True):
        self.ops.append((waits, fn, sig))
        if not sig:
            return None
        self.n += 1
        return (self.sem, self.n)


def flat(waits):
    for w in waits:
        if w is None:
            continue
        if isinstance(w, list):
            yield from flat(w)
        else:
            yield w


def run_queue(eng, queue):
    seen = {}
    for waits, fn, sig in queue.ops:
        need = {}
        for sem, value in flat(waits):
            if value > max(seen.get(id(sem), 0), need.get(id(sem), (None, 0))[1]):
                need[id(sem)] = (sem, value)
        for key, (sem, value) in need.items():
            eng.wait_ge(sem, value)
            seen[key] = value
        ins = fn(eng)
        if sig is True:
            ins.then_inc(queue.sem, 1)
        elif sig:
            ins.then_inc(sig, 16)


def build(nc, x_d, w_d, cst_d, s5_d, att_d, msk_d, out_d):
    n_units = w_d.shape[0]
    sem = {n: nc.alloc_semaphore(n) for n in ("pe", "act", "dve", "pool", "s_cst", "s_s5", "s_att", "s_msk",
                                              "s_w3", "s_out")}
    ds = [nc.alloc_semaphore(f"ds{i}") for i in range(NR)]
    dx = [nc.alloc_semaphore(f"dx{i}") for i in range(KD)]
    pe, act, dve, pool = (Queue(sem[n]) for n in ("pe", "act", "dve", "pool"))
    sp = Queue(None)

    top = [1152]

    def at(name, shape, dt, offset=None):
        size = math.prod(shape[1:]) * (1 if dt == U8 else 4)
        if offset is None:
            offset = top[0]
            top[0] += (size + 31) // 32 * 32
        return nc.alloc_sbuf_tensor_at(name, list(shape), dt, offset=offset)

    X = at("X", [P, KD, T], F32)
    Hh = at("Hh", [P, KD, T], F32R)
    Hl = at("Hl", [P, KD, T], F32R)
    wraw = at("wraw", [P, NR, 1024], F32)
    whi = at("whi", [P, NH, 1024], F32R)
    wlo = at("wlo", [P, NH, 1024], F32R)
    cst = at("cst", [P, NCOLS], F32)
    msk = at("msk", [P, 8, P], U8)
    ones = at("ones", [P, P], F32)
    epsc = at("epsc", [P, 4], F32)
    gh = at("gh", [P, 16], F32)
    rcol = at("rcol", [P, 48], F32)
    hcol = at("hcol", [P, 32], F32)
    small = at("small", [P, 64], F32)
    acc = at("acc", [P, T], F32)
    zsum = at("zsum", [P, T], F32)
    Rb = at("Rb", [P, T], F32)
    MUb = at("MUb", [P, T], F32)
    tmp = [at(f"tmp{i}", [P, T], F32) for i in range(4)]
    tmp.append(at("tmp4", [P, T], F32))
    dgt = at("dgt", [P, 4, P], F32)
    identr = at("identr", [P, P], F32R)
    colr = at("colr", [P, 6, 2, 4], F32R)
    zeros = at("zeros", [P, 16], F32)
    sq = at("sq", [P, T], F32)
    Bre = at("Bre", [P, 16, 16], F32)
    Bim = at("Bim", [P, 16, 16], F32)
    pw = at("pw", [P, 5, 9, 16], F32)
    sp5 = at("sp5", [P, 16, 16], F32)
    M8 = at("M8", [P, 2, 32], F32)
    arena = top[0]
    cur = [arena]

    def ar(name, shape, dt, offset=None):
        size = math.prod(shape[1:]) * 4
        if offset is None:
            offset = cur[0]
            cur[0] += size
        assert offset + size <= 229344, (name, offset + size)
        return nc.alloc_sbuf_tensor_at(name, list(shape), dt, offset=offset), offset

    Ah, _ = ar("Ah", [P, NF, T], F32R)
    Al, _ = ar("Al", [P, NF, T], F32R)
    Y, _ = ar("Y", [P, KD, T], F32)
    cur[0] = arena
    Qf, _ = ar("Qf", [P, 4, T], F32)
    Kf, _ = ar("Kf", [P, 4, T], F32)
    Vt, _ = ar("Vt", [P, 4, T], F32)
    PT, o_pt = ar("PT", [P, 4, T], F32)
    U2, o_u2 = ar("U2", [P, 32, 4, 16], F32)
    cur[0] += 8192
    Up, o_up = ar("Up", [P, 32, 64], F32)
    W1, o_w1 = ar("W1", [P, 16, 2, 2, 64], F32)
    G2, _ = ar("G2", [P, 32, 9, 16], F32)
    Wri, o_wr = ar("Wri", [P, 2, 16, 8, 16], F32)
    W3, _ = ar("W3", [P, 32, P], F32, o_u2)
    yh, _ = ar("yh", [P, 4, T], F32R, o_u2)
    yl, _ = ar("yl", [P, 4, T], F32R, o_u2 + 8192)
    yg, _ = ar("yg", [P, 4, T], F32, o_up)
    Kr, _ = ar("Kr", [P, 32, P], F32, o_w1)
    Y2, _ = ar("Y2", [P, 8, T], F32, o_w1)
    FS, _ = ar("FS", [P, 64, 2, 16], F32, o_wr)
    XS, _ = ar("XS", [P, 64, 2, 16], F32, o_wr + 8192)
    Wt, _ = ar("Wt", [P, 16, 8, 16], F32, o_pt)
    Ga, _ = ar("Ga", [P, 16, 9, 16], F32, o_pt)
    Gt, _ = ar("Gt", [P, 16, 9, 16], F32, o_pt + 9216)
    XS2, _ = ar("XS2", [P, 64, 32], F32, o_wr)
    cur[0] = arena
    QP, o_qp = ar("QP", [P, 4, T], F32)
    KS, o_ks = ar("KS", [P, 4, T], F32)
    Ph, _ = ar("Ph", [P, 4, T], F32R, o_qp)
    Pl, _ = ar("Pl", [P, 4, T], F32R, o_ks)
    FT, _ = ar("FT", [P, 4, T], F32)
    TT, _ = ar("TT", [P, 4 * T], F32)
    V2, _ = ar("V2", [P, 4, T], F32)
    Sc, _ = ar("Sc", [P, 4, 4, T], F32)
    Sg, _ = ar("Sg", [P, 4, T], F32)
    Oh, _ = ar("Oh", [P, 4, T], F32)
    U3, _ = ar("U3", [P, 4, 16 + T], F32)
    PA, _ = ar("PA", [P, 2, 16 + T], F32)
    Dp, Cn = zsum, MUb

    bank_t = [nc.alloc_psum_tensor(f"bank{i}", [P, T], F32) for i in range(8)]
    bfree = [[] for _ in range(8)]
    bnext = [0]

    def bank():
        while bfree[bnext[0] % 8] is None:
            bnext[0] += 1
        i = bnext[0] % 8
        bnext[0] += 1
        w = bfree[i]
        bfree[i] = None
        return i, bank_t[i], w

    def c(name, i=None, n=1):
        a, b = COLS[name]
        return cst[:, a:b] if i is None else cst[:, a + i:a + i + n]

    ident = c("ident")

    def mm(out, lhsT, rhs, start, stop, *waits, sig=False, skip=False):
        return pe(lambda e: e.matmul(out, lhsT, rhs, start=start, stop=stop, skip_group_check=skip),
                  *waits, sig=sig)

    def tr(out, in_, idn, *waits, sig=False):
        return pe(lambda e: e.transpose(out, in_, idn), *waits, sig=sig)

    def A(out, in_, func, *waits, **kw):
        return act(lambda e: e.activation(out, in_, func, **kw), *waits)

    def tt(q, out, a, b, op, *waits):
        return q(lambda e: e.tensor_tensor(out, a, b, op), *waits)

    def ts(q, out, a, s1, s2, op0, op1, *waits):
        if op1 is None:
            return q(lambda e: e.tensor_scalar(out, a, s1, None, op0), *waits)
        return q(lambda e: e.tensor_scalar(out, a, s1, s2, op0, op1), *waits)

    def stt(out, a, s, b, op0, op1, *waits, **kw):
        return dve(lambda e: e.scalar_tensor_tensor(out, a, s, b, op0, op1, **kw), *waits)

    def f32(ap):
        return ap.bitcast(F32)

    hi_done = {}
    lo_done = {}
    unit_used = {}
    pos = [0]
    late = [False]

    def load(u):
        if u < n_units:
            sp(lambda e: e.dma_start(wraw[:, u % NR, :], w_d[u]), lo_done.get(u - NR), sig=ds[u % NR])

    def prep_hi(u):
        if u >= n_units or u in hi_done:
            return
        hi_done[u] = A(whi[:, u % NH, :], wraw[:, u % NR, :], ACT.Copy, (ds[u % NR], 16 * (u // NR + 1)),
                       unit_used.get(u - NH))

    def prep_lo(u, q=dve):
        if u >= n_units or u in lo_done:
            return
        lo_done[u] = tt(q, wlo[:, u % NH, :], wraw[:, u % NR, :], f32(whi[:, u % NH, :]), SUB, hi_done[u])
        load(u + NR)

    def prep(u, q=dve):
        prep_hi(u)
        prep_lo(u, q)

    def finish_preps():
        for u in hi_done:
            prep_lo(u)

    def prep_ahead():
        if pos[0] % 8 == 0:
            prep(pos[0] // 8 + AHEAD, pool)

    def wtile(n=1):
        i = pos[0]
        u, t = i // 8, i % 8
        if t == 0:
            prep_hi(u + AHEAD)
            if not late[0]:
                prep_lo(u + AHEAD)
        if t == 4:
            prep_lo(u + AHEAD)
        pos[0] += n
        h = u % NH
        return whi[:, h, t * P:(t + n) * P], wlo[:, h, t * P:(t + n) * P], lo_done[u], (u if t + n == 8 else None)

    def mm3(out, sh, sl, mh, ml, start, stop, waits, hw, unit, sig=False):
        mm(out, sh, mh, start, False, hw[0], *waits)
        mm(out, sl, mh, False, False)
        t = mm(out, sh, ml, False, stop, hw[1], sig=sig or unit is not None)
        if unit is not None:
            unit_used[unit] = t
        return t

    def gemm_group(mh, ml, hw, mid=None):
        banks = [bank() for _ in range(4)]
        for k in range(KD):
            if k == 0:
                tiles = [wtile() for i in range(4)]
                for i, (hi, lo, w, unit) in enumerate(tiles):
                    mm(banks[i][1][:, :], hi, mh[:, 0, :], True, False, w, hw[0][0], banks[i][2])
                    mm(banks[i][1][:, :], lo, mh[:, 0, :], False, False)
                for i, (hi, lo, w, unit) in enumerate(tiles):
                    t = mm(banks[i][1][:, :], hi, ml[:, 0, :], False, False, hw[0][1], sig=unit is not None)
                    if unit is not None:
                        unit_used[unit] = t
            for i in range(4 if k else 0):
                hi, lo, w, unit = wtile()
                last = k == KD - 1
                t = mm3(banks[i][1][:, :], hi, lo, mh[:, k, :], ml[:, k, :], False, last, [w], hw[k], unit, sig=last and i == 3)
            if mid is not None:
                mid(k)
        finish_preps()
        return [b[0] for b in banks], t

    def gemm_tokens(toks, hw, mid=None):
        banks = [bank() for _ in range(4)]
        for k in range(KD):
            hi, lo, w, unit = wtile(4)
            last = k == KD - 1
            for m in range(4):
                mm(banks[m][1][:, :], toks(Hh, k, m), hi, k == 0, False, w, hw[k][0], banks[m][2] if k == 0 else None)
                mm(banks[m][1][:, :], toks(Hh, k, m), lo, False, False)
                t = mm(banks[m][1][:, :], toks(Hl, k, m), hi, False, last, hw[k][1],
                       sig=m == 3 and (last or unit is not None))
            if unit is not None:
                unit_used[unit] = t
            if mid is not None:
                mid(k)
        finish_preps()
        return [b[0] for b in banks], t

    def gemm_row(nk, mh, ml, mw, mid=None):
        i, b, w0 = bank()
        for k in range(nk):
            hi, lo, w, unit = wtile()
            t = mm3(b[:, :], hi, lo, mh[:, k, :], ml[:, k, :], k == 0, k == nk - 1,
                    [w, w0 if k == 0 else None], mw[k], unit, sig=k == nk - 1)
            if mid is not None:
                mid(k)
        return i, t

    def half_rows(mh, ml, mw):
        held = []
        for nb in range(4):
            i, b, w0 = bank()
            for k in range(4):
                hi, lo, w, unit = wtile()
                mm3(b[:, :], hi, lo, mh[:, k, :], ml[:, k, :], k == 0, False, [w, w0 if k == 0 else None], mw[k],
                    unit)
            held.append((i, b))
        return held

    def gemm_rows(nk, mh, ml, mw, held, mid=None):
        for nb in range(KD):
            if nb < len(held):
                i, b = held[nb]
                for k in range(4, 8):
                    hi, lo, w, unit = wtile()
                    t = mm3(b[:, :], hi, lo, mh[:, k, :], ml[:, k, :], False, k == 7, [w], mw[k], unit, sig=k == 7)
                    if mid is not None:
                        mid(k, nb)
            else:
                i, t = gemm_row(nk, mh, ml, mw, lambda k: mid(k, nb) if mid is not None else None)
            if nb == KD - 1:
                finish_preps()
            yield i, t

    load(0)
    sp(lambda e: e.dma_start(cst[:, :], cst_d), sig=sem["s_cst"])
    for k in range(KD):
        sp(lambda e, k=k: e.dma_start(X[:, k, :], x_d[:, k, :]), sig=dx[k])
        if k in (2, 5):
            load(k // 2)
    sp(lambda e: e.dma_start(MUb[:, :], s5_d[:, 1, :]), sig=sem["s_s5"])
    sp(lambda e: e.dma_start(Y[:, 0:2, :], msk_d), sig=sem["s_msk"])
    cst_in = (sem["s_cst"], 16)
    ones_in = pool(lambda e: e.memset(ones[:, :], 1.0))
    pool(lambda e: e.memset(epsc[:, 0:1], 1e-6))
    pool(lambda e: e.memset(epsc[:, 1:2], 1e-5))
    eps_in = pool(lambda e: e.memset(epsc[:, 2:3], math.pi / 2))
    zeros_in = pool(lambda e: e.memset(zeros[:, :], 0.0))
    identr_in = A(identr[:, :], ident, ACT.Copy, cst_in)
    gh_in = ts(dve, gh[:, 0:8], c("g_f1post"), 0.5, None, MUL, None, cst_in)
    gh_in = ts(dve, gh[:, 8:16], c("g_f2post"), 0.5, None, MUL, None, cst_in)

    state = {"x": [(dx[k], 16) for k in range(KD)], "h_used": None, "acc_used": None, "zsum_used": None,
             "tmp": [None] * 5, "colr": [None] * 6, "Rb_used": None, "MUb_used": None, "arena": None,
             "sq_used": None, "y_free": None}

    def split_h(k, src, scale, ready):
        if scale is None:
            hi = A(Hh[:, k, :], src, ACT.Copy, ready, state["h_used"])
            lo = tt(dve, Hl[:, k, :], src, f32(Hh[:, k, :]), SUB, hi, ready, state["h_used"])
        else:
            hi = A(Hh[:, k, :], src, ACT.Copy, ready, state["h_used"], cst_in, scale=scale)
            lo = stt(Hl[:, k, :], src, scale, f32(Hh[:, k, :]), MUL, SUB, hi, ready, state["h_used"], cst_in)
        return [hi, lo]

    def square(src, k, ready):
        if k == KD - 1:
            state["sq"] = A(sq[:, :], src, ACT.Square, ready, state["sq_used"])
        elif k == 0:
            state["acc"] = A(acc[:, :], src, ACT.Square, ready, state["acc_used"])
        else:
            i, b, w0 = bank()
            s = A(b[:, :], src, ACT.Square, ready, w0)
            state["acc"] = tt(dve, acc[:, :], b[:, :], acc[:, :], ADD, s, state["acc"])
            bfree[i] = [state["acc"]]

    def zero_cols(b, w0):
        mm(b[:, 0:16], ident, zeros[:, :], True, False, cst_in, zeros_in, w0, skip=True)

    def col_sums(src, b, col, ready, perm=False):
        for m in range(4):
            lhsT = src[:, m::4] if perm else src[:, m * P:(m + 1) * P]
            t = mm(b[:, col + 2 * m:col + 2 * m + 2], lhsT, ones[:, 0:2], False, m == 3, ready, ones_in, sig=m == 3, skip=True)
        return t

    def spread(cols, ready, b, w0, slot=0):
        return spread_mm(spread_cols(cols, ready, slot), b, w0)

    def spread_cols(cols, ready, slot=0):
        c1 = ts(dve, colr[:, slot, 0, :], cols, 1.0, None, MUL, None, ready, state["colr"][slot])
        c2 = tt(dve, colr[:, slot, 1, :], cols, f32(colr[:, slot, 0, :]), SUB, c1)
        return c1, c2, slot

    def spread_mm(made, b, w0):
        c1, c2, slot = made
        for m in range(4):
            for part, c_ in ((0, c1), (1, c2)):
                t = mm(b[:, m * P:(m + 1) * P], colr[:, slot, part, m:m + 1].to_broadcast([P, P]), identr[:, :],
                       part == 0, part == 1, c_, w0, identr_in, sig=m == 3 and part == 1, skip=True)
        state["colr"][slot] = t
        return t, c2

    def sqrt_table():
        A(epsc[:, 3:4], epsc[:, 0:1], ACT.Sqrt, eps_in)

    def rms_cols(perm):
        i, b, w0 = bank()
        zero_cols(b, w0)
        for src in ("acc", "sq"):
            for p_ in range(2 if perm else 1):
                t = col_sums({"acc": acc, "sq": sq}[src][:, :], b, 8 * p_, state[src], p_ == 1)
        state["acc_used"] = state["sq_used"] = t
        n = 8 if perm else 4
        v = A(small[:, 0:n], b[:, 0:2 * n:2], ACT.Sqrt, t, eps_in, state.get("small_used"), scale=1.0 / D,
              bias=epsc[:, 0:1])
        r = dve(lambda e: e.reciprocal(rcol[:, 0:n], small[:, 0:n]), v, state.get("rcol_used"))
        bfree[i] = [v]
        state["small_used"] = r
        return r

    def rms_spread(perm=False):
        r = rms_cols(perm)
        made = spread_cols(rcol[:, 0:4], r)
        yield
        i, b, w0 = bank()
        t, dg = spread_mm(made, b, w0)
        state["rcol_used"] = dg
        cp = A(Rb[:, :], b[:, :], ACT.Copy, t, state["Rb_used"])
        bfree[i] = [cp]
        state["rms"] = r, cp
        yield

    def pre_norm(g, k, ready):
        h = split_h(k, X[:, k, :], c(g, k), ready)
        if k in (0, KD - 1):
            square(X[:, k, :], k, ready)
        else:
            q = tt(pool, zsum[:, :], X[:, k, :], X[:, k, :], MUL, ready, state["zsum_used"])
            state["acc"] = state["zsum_used"] = tt(pool, acc[:, :], acc[:, :], zsum[:, :], ADD, q, state["acc"])
        return h

    def post_norm(g, ycp, then):
        r = rms_cols(False)
        prep_ahead()
        i, b, w0 = bank()
        t, dg = spread(rcol[:, 0:4], r, b, w0)
        state["rcol_used"] = dg
        bb = [bank(), bank()]
        used = [bb[0][2], bb[1][2]]
        hw = []
        for k in range(KD):
            bk = bb[k % 2][1]
            a = tt(dve, bk[:, :], Y[:, k, :], b[:, :], MUL, t, ycp[k], used[k % 2])
            x = stt(X[:, k, :], bk[:, :], g(k), X[:, k, :], MUL, ADD, a, gh_in, cst_in, state["x"][k])
            used[k % 2] = x
            state["x"][k] = x
            if k:
                hw.append(then(k - 1, state["x"][k - 1]))
        hw.append(then(KD - 1, x))
        bfree[i] = [a]
        for j in range(2):
            bfree[bb[j][0]] = [used[j]]
        state["y_free"] = a
        return hw

    later = []

    def scale_x(hw):
        state["x"] = [A(X[:, k, :], X[:, k, :], ACT.Copy, hw[k], scale=ALPHA) for k in range(KD)]

    def ffn_in(hw, rsp):
        aw = []
        rs = None
        for j in range(0, NF, 2):
            def beside_in(k):
                if j and k in (2, 5):
                    next(side, None)
                if j == 0 and rsp is not None and k > 5:
                    next(rsp)

            banks, t = gemm_group(Hh, Hl, hw, beside_in)
            if rsp is not None:
                rs = state["rms"][1]
            if j == 2 and later:
                later.pop()()
            g = [bank_t[banks[i]] for i in range(2)]
            u = [bank_t[banks[2 + i]] for i in range(2)]
            s, v = tmp[0:2], tmp[2:4]
            tu = state["tmp"]
            if rs is not None:
                m1 = [tt(dve, s[i][:, :], g[i][:, :], Rb[:, :], MUL, t, rs, tu[i]) for i in range(2)]
                s1 = [A(s[i][:, :], s[i][:, :], ACT.Silu, m1[i]) for i in range(2)]
                s2 = [tt(pool, s[i][:, :], s[i][:, :], Rb[:, :], MUL, s1[i]) for i in range(2)]
                gfree = m1
                state["Rb_used"] = [m1, s2]
            else:
                s2 = [A(s[i][:, :], g[i][:, :], ACT.Silu, t, tu[i]) for i in range(2)]
                gfree = s2
            m2 = [tt(dve, v[i][:, :], u[i][:, :], s[i][:, :], MUL, t, s2[i], tu[2 + i]) for i in range(2)]
            hi = [A(Ah[:, j + i, :], v[i][:, :], ACT.Copy, m2[i], state["arena"]) for i in range(2)]
            lo = [tt(dve, Al[:, j + i, :], v[i][:, :], f32(Ah[:, j + i, :]), SUB, hi[i], state["arena"])
                  for i in range(2)]
            for i in range(2):
                tu[i] = m2[i]
                tu[2 + i] = lo[i]
                bfree[banks[i]] = [gfree[i]]
                bfree[banks[2 + i]] = [m2[i]]
                aw.append([hi[i], lo[i]])
            next(side, None)
        state["h_used"] = t
        return aw

    def out_rms(nk, mh, ml, mw, held=()):
        ycp = []
        for nb, (i, t) in enumerate(gemm_rows(nk, mh, ml, mw, held)):
            if nb == KD - 1:
                sqrt_table()
                square(bank_t[i][:, :], nb, t)
            cp = A(Y[:, nb, :], bank_t[i][:, :], ACT.Copy, t, state.get("y_free"), state["arena"])
            bfree[i] = [cp]
            ycp.append(cp)
            if nb < KD - 1:
                square(Y[:, nb, :], nb, cp)
        return ycp, t

    def out_ln(nk, mh, ml, mw, half, li, last=False, held=()):
        zc = []
        sh = {}

        def centre():
            i, b, w0 = bank()
            zero_cols(b, w0)
            t = col_sums(zsum[:, :], b, 0, sh["z1"])
            cm = ts(dve, rcol[:, 16:20], b[:, 0:8:2], 1.0 / 256, None, MUL, None, t, state.get("mcol_used"))
            ch = ts(dve, rcol[:, 20:24], b[:, 0:8:2], 1.0 / 512, None, MUL, None, t, state.get("mcol_used"))
            bfree[i] = [ch]
            sh["mcol"] = cm
            sh["half"] = ch
            sh["zt"] = [sh["zt"], t]

        def centre_2():
            i, b, w0 = bank()
            t, dg = spread(rcol[:, 16:20], sh["mcol"], b, w0)
            mu = A(MUb[:, :], b[:, :], ACT.Copy, t, state["MUb_used"])
            bfree[i] = [mu]
            for k in range(4, KD):
                state["x"][k] = tt(pool, X[:, k, :], X[:, k, :], MUb[:, :], SUB, mu, state["x"][k])
            sh["mu"] = mu

        def mid(k, nb):
            if nb == 2 and k == nk // 2:
                centre()
            if nb == 3 and k == nk // 2 + 1:
                centre_2()
            if nb == 7 and k == nk - 2:
                sh["sums"] = [bank(), bank()]
                for (_, b, w0), src, ready in zip(sh["sums"], (zsum, acc), (sh["zt"], state["acc"])):
                    zero_cols(b, w0)
                    col_sums(src[:, :], b, 0, ready)

        for nb, (i, t) in enumerate(gemm_rows(nk, mh, ml, mw, held, mid)):
            if nb == KD - 1:
                sqrt_table()
            z = stt(Y[:, nb, :], bank_t[i][:, :], half, X[:, nb, :], MUL, ADD, t, state["x"][nb],
                    state.get("y_free"), state["arena"])
            bfree[i] = [z]
            if nb == 1:
                sh["zt"] = sh["z1"] = tt(pool, zsum[:, :], Y[:, 0, :], Y[:, 1, :], ADD, zc[0], z, state["zsum_used"])
            elif 1 < nb < 7:
                sh["zt"] = tt(pool, zsum[:, :], zsum[:, :], Y[:, nb, :], ADD, sh["zt"], z)
            zc.append(z)
            if nb == 3:
                for k in range(4):
                    zc[k] = tt(dve, Y[:, k, :], Y[:, k, :], MUb[:, :], SUB, zc[k], sh["mu"], sh["zt"])
                    square(Y[:, k, :], k, zc[k])
                state["MUb_used"] = [state["x"][7], zc[3]]
            elif nb > 3:
                square(Y[:, nb, :], nb, z)
        gemm_end = t
        (i, b, _), (i_, b_, _) = sh["sums"]
        t1 = col_sums(Y[:, 7, :], b, 0, zc[7])
        t2 = col_sums(sq[:, :], b_, 0, state["sq"])
        state["zsum_used"] = state["acc_used"] = state["sq_used"] = t2
        su = state.get("small_used")
        def rest(k):
            hi, x = hw[k]
            lo = tt(dve, Hl[:, k, :], X[:, k, :], f32(Hh[:, k, :]), SUB, hi, x, state["h_used"])
            hw[k] = [hi, lo]

        d1 = stt(small[:, 0:4], b[:, 0:8:2], 1.0 / D, rcol[:, 20:24], MUL, SUB, t1, sh["half"], su)
        d2 = tt(dve, small[:, 4:8], small[:, 0:4], small[:, 0:4], MUL, d1)
        i1, b1, w1 = bank()
        td, dg = spread(small[:, 0:4], d1, b1, w1, 1)
        d3 = stt(small[:, 8:12], b_[:, 0:8:2], 1.0 / D, small[:, 4:8], MUL, SUB, t2, d2)
        bfree[i] = [d1]
        bfree[i_] = [d3]
        sd = A(small[:, 12:16], small[:, 8:12], ACT.Sqrt, d3, eps_in, bias=epsc[:, 1:2])
        def centred(k):
            return tt(dve, Y[:, k, :], Y[:, k, :], b1[:, :], SUB, td, zc[k], state["sq"], state["acc"], t1)

        r = dve(lambda e: e.reciprocal(rcol[:, 0:4], small[:, 12:16]), sd, state.get("rcol_used"))
        if not last:
            prep_ahead()
        i2, b2, w2 = bank()
        tr_, dg = spread(rcol[:, 0:4], r, b2, w2)
        a = [centred(k) for k in range(EARLY + last)]
        state["rcol_used"] = state["mcol_used"] = state["small_used"] = dg
        hw = []
        for k in range(KD):
            lg, lb_ = c("ln_g", li * 8 + k), c("ln_b", li * 8 + k)
            if k >= EARLY + last:
                a.append(centred(k))
            n = tt(dve, Y[:, k, :], Y[:, k, :], b2[:, :], MUL, tr_, a[k])
            if not last:
                hi = A(Hh[:, k, :], Y[:, k, :], ACT.Identity, n, cst_in, state["h_used"], scale=lg, bias=lb_)
            x = A(X[:, k, :], Y[:, k, :], ACT.Identity, n, zc, cst_in, scale=lg, bias=lb_)
            if last:
                sp(lambda e, k=k: e.dma_start(out_d[:, k, :], X[:, k, :]), x, sig=sem["s_out"])
                continue
            hw.append([hi, x])
            if k:
                rest(k - 1)
        bfree[i1] = [a[KD - 1]]
        bfree[i2] = [n]
        if not last:
            rest(KD - 1)
            later.append(lambda: scale_x(hw))
        state["y_free"] = x
        return hw, gemm_end

    def s5_small():
        a_re, a_im, ldt = c("a_re"), c("a_im"), c("log_dt")

        def S(i):
            return sp5[:, i, :]

        s5_in = (sem["s_s5"], 32)
        seq = [None]

        def v(fn):
            seq[0] = dve(fn, seq[0], cst_in)
            return seq[0]

        def vtt(o, a, b, op):
            return v(lambda e: e.tensor_tensor(o, a, b, op))

        def vts(o, a, s1, s2, op0, op1=None):
            if op1 is None:
                return v(lambda e: e.tensor_scalar(o, a, s1, None, op0))
            return v(lambda e: e.tensor_scalar(o, a, s1, s2, op0, op1))

        def vstt(o, a, s, b, op0, op1):
            return v(lambda e: e.scalar_tensor_tensor(o, a, s, b, op0, op1))

        t = A(S(0), ldt, ACT.Exp, cst_in)
        seq[0] = t
        yield
        vtt(S(1), S(0), a_re, MUL)
        t = vtt(S(2), S(0), a_im, MUL)
        mag = A(S(3), S(1), ACT.Exp, t)
        magic = 1.5 * 2.0 ** 23
        vts(S(4), S(2), 1.0 / (2 * math.pi), magic, MUL, ADD)
        vts(S(4), S(4), magic, None, SUB)
        yield
        c1 = 6.28125
        c2 = 0.00193500518798828125
        c3 = 2 * math.pi - c1 - c2
        vstt(S(5), S(4), -c1, S(2), MUL, ADD)
        vstt(S(5), S(4), -c2, S(5), MUL, ADD)
        vstt(S(5), S(4), -c3, S(5), MUL, ADD)
        t = vts(S(5), S(5), math.pi, -math.pi, ALU.min, ALU.max)
        yield
        sn = A(S(6), S(5), ACT.Sin, t, scale=0.5)
        cs = A(S(7), S(5), ACT.Sin, t, eps_in, scale=-0.5, bias=epsc[:, 2:3])
        seq[0] = [sn, cs, mag]
        yield
        vstt(S(8), S(6), 2.0, S(7), MUL, MUL)
        vstt(S(9), S(6), -2.0, S(6), MUL, MUL)
        vts(S(9), S(9), 1.0, None, ADD)

        def PW(i, m):
            return pw[:, i, m, :]

        v(lambda e: e.memset(PW(0, 0), 1.0))
        v(lambda e: e.memset(PW(1, 0), 0.0))
        vtt(PW(0, 1), S(3), S(9), MUL)
        vtt(PW(1, 1), S(3), S(8), MUL)
        for m in range(2, 9):
            vtt(S(10), PW(0, m - 1), PW(0, 1), MUL)
            vtt(S(11), PW(1, m - 1), PW(1, 1), MUL)
            vtt(PW(0, m), S(10), S(11), SUB)
            vtt(S(10), PW(0, m - 1), PW(1, 1), MUL)
            vtt(S(11), PW(1, m - 1), PW(0, 1), MUL)
            vtt(PW(1, m), S(10), S(11), ADD)
            yield
        vts(pw[:, 2, :, :], pw[:, 1, :, :], -1.0, None, MUL)
        for m in range(8):
            vts(PW(3, m), PW(0, 7 - m), 1.0, None, MUL)
            vts(PW(4, m), PW(1, 7 - m), 1.0, None, MUL)
            if m % 4 == 3:
                yield
        vts(M8[:, 0, 0:16], PW(0, 8), 1.0, None, MUL)
        vts(M8[:, 0, 16:32], PW(2, 8), 1.0, None, MUL)
        vts(M8[:, 1, 0:16], PW(1, 8), 1.0, None, MUL)
        vts(M8[:, 1, 16:32], PW(0, 8), 1.0, None, MUL)
        yield
        vts(S(10), PW(0, 1), -1.0, None, ADD)
        vtt(S(11), a_re, a_re, MUL)
        vtt(S(12), a_im, a_im, MUL)
        vtt(S(11), S(11), S(12), ADD)
        v(lambda e: e.reciprocal(S(12), S(11)))
        yield
        vtt(S(13), S(10), a_re, MUL)
        vtt(S(14), PW(1, 1), a_im, MUL)
        vtt(S(13), S(13), S(14), ADD)
        vtt(S(13), S(13), S(12), MUL)
        yield
        vtt(S(14), PW(1, 1), a_re, MUL)
        vtt(S(15), S(10), a_im, MUL)
        vtt(S(14), S(14), S(15), SUB)
        vtt(S(14), S(14), S(12), MUL)
        yield
        wr = S(13).unsqueeze(2).to_broadcast([P, 16, 16])
        wi = S(14).unsqueeze(2).to_broadcast([P, 16, 16])
        bre = tmp[4][:, 0:256].rearrange("p (a b) -> p a b", b=16)
        bim = tmp[4][:, 256:512].rearrange("p (a b) -> p a b", b=16)
        t3 = dgt[:, 0:2, :].rearrange("p a b -> p (a b)").rearrange("p (a b) -> p a b", b=16)
        seq[0] = [seq[0], s5_in]
        vtt(Bre[:, :, :], wr, bre, MUL)
        vtt(t3, wi, bim, MUL)
        vtt(Bre[:, :, :], Bre[:, :, :], t3, SUB)
        yield
        vtt(Bim[:, :, :], wr, bim, MUL)
        vtt(t3, wi, bre, MUL)
        t = vtt(Bim[:, :, :], Bim[:, :, :], t3, ADD)
        state["tmp"][4] = t
        B2 = dgt[:, :, :].rearrange("p a b -> p (a b)")
        for g2 in range(2):
            for ri, src in enumerate((Bre, Bim)):
                dst = B2.rearrange("p (a g n) -> p a g n", g=2, n=16)[64 * ri:64 * ri + 64, :, g2, :]
                state.setdefault("b2_in", []).append(
                    A(dst, src[64 * g2:64 * g2 + 64, :, :], ACT.Copy, t))
        state["s5_in"] = t

    def s5_big(small_in):
        af = [state["arena"], small_in]

        def powers(i, n):
            return pw[:, i, 0:n, :].rearrange("p m a -> p a m").unsqueeze(3).to_broadcast([P, 16, n, 16])

        def chans(ap, n):
            return ap.unsqueeze(2).to_broadcast([P, 16, n, 16])

        seq = [af]

        def p(o, a, b, op):
            done = []
            for pr, q in ((0, dve), (8, pool), (4, dve), (12, pool)):
                done.append(q(lambda e, pr=pr: e.tensor_tensor(o[:, pr:pr + 4], a[:, pr:pr + 4], b[:, pr:pr + 4], op),
                              *seq))
            seq[0] = done

        wre, wim = Wri[:, 0], Wri[:, 1]
        rr, ri = powers(3, 8), powers(4, 8)
        br, bi = chans(Bre[:, :, :], 8), chans(Bim[:, :, :], 8)
        p(wre, rr, br, MUL)
        yield
        p(Wt[:, :, :, :], ri, bi, MUL)
        yield
        p(wre, wre, Wt[:, :, :, :], SUB)
        yield
        p(wim, rr, bi, MUL)
        yield
        p(Wt[:, :, :, :], ri, br, MUL)
        yield
        p(wim, wim, Wt[:, :, :, :], ADD)
        state["w_in"] = seq[0]

    def s5_big2(u2_read):
        def powers(i, n):
            return pw[:, i, 0:n, :].rearrange("p m a -> p a m").unsqueeze(3).to_broadcast([P, 16, n, 16])

        seq = [[u2_read, state["w_in"], state["arena"]]]

        def p(o, a, b, op):
            done = []
            for pr, q in ((0, dve), (8, pool), (4, dve), (12, pool)):
                done.append(q(lambda e, pr=pr: e.tensor_tensor(o[:, pr:pr + 4], a[:, pr:pr + 4], b[:, pr:pr + 4], op),
                              *seq))
            seq[0] = done

        def by_group(ri):
            done = []
            for g2 in range(2):
                for pr in range(0, 16, 4):
                    r = slice(64 * g2, 64 * g2 + 64)
                    dst = G2[64 * ri:64 * ri + 64, 2 * pr + g2:2 * pr + 8:2, :, :]
                    q = pool if g2 == ri and pr >= 8 else dve
                    done.append(q(lambda e, r=r, pr=pr, dst=dst: e.tensor_tensor(
                        dst, Ga[r, pr:pr + 4, :, :], Gt[r, pr:pr + 4, :, :], SUB), *seq))
            seq[0] = done

        cr = MUb[:, 0:256].rearrange("p (a b) -> p a b", b=16).unsqueeze(2).to_broadcast([P, 16, 9, 16])
        ci = MUb[:, 256:512].rearrange("p (a b) -> p a b", b=16).unsqueeze(2).to_broadcast([P, 16, 9, 16])
        ga, gt = Ga[:, :, :, :], Gt[:, :, :, :]
        p(ga, powers(0, 9), cr, MUL)
        yield
        p(gt, powers(1, 9), ci, MUL)
        yield
        by_group(0)
        first = seq[0]
        yield
        p(ga, powers(2, 9), cr, MUL)
        yield
        p(gt, powers(0, 9), ci, MUL)
        yield
        by_group(1)
        state["g_in"] = [first, seq[0]]

    def mixer_1(hw):
        s5_in, b2_in = state["s5_in"], state["b2_in"]
        B2 = dgt[:, :, :].rearrange("p a b -> p (a b)")
        late[0] = True
        big = s5_big(s5_in)
        rsp = rms_spread(perm=True)

        def beside_u(k):
            if k > 1:
                next(big, None)
            if k > 5:
                next(rsp)

        banks, t = gemm_tokens(lambda h, k, m: h[:, k, m::4], hw, beside_u)
        rc, rb = state["rms"]
        for _ in big:
            pass
        w_in = state["w_in"]
        u2 = []
        for m in range(4):
            b = bank_t[banks[m]]
            e = A(U2[:, :, m, :], b[:, :].rearrange("p (g n) -> p g n", n=16), ACT.Copy, t, rc, state["arena"],
                  scale=rcol[:, 4 + m:5 + m])
            bfree[banks[m]] = [e]
            u2.append(e)
        ups, w1 = [], []

        def turn_u(q):
            i, b, w0 = bank()
            for s in range(4):
                t = tr(b[0:64, s * P:(s + 1) * P], U2[:, 4 * q + s, :, :], ident, u2, w0, cst_in, sig=s == 3)
            src = b[0:64, :].rearrange("p (g j s) -> p g j s", g=4, s=2)
            e1 = A(Up[0:64, 4 * q:4 * q + 4, :], src[:, :, :, 0], ACT.Copy, t, state["arena"])
            e2 = A(Up[64:128, 4 * q:4 * q + 4, :], src[:, :, :, 1], ACT.Copy, t, state["arena"])
            bfree[i] = [e2]
            ups.append(e2)
            return t

        def turn_w(q):
            i, b, w0 = bank()
            for s in range(4):
                t = tr(b[:, s * P:(s + 1) * P], Wri[:, s % 2, 2 * q + s // 2, :, :], ident, w_in, w0, cst_in,
                       sig=s == 3)
            for s in range(2):
                src = b[:, s * 256:(s + 1) * 256].rearrange("p (r g q) -> p g r q", r=2, g=2)
                if q % 2:
                    e = A(W1[:, 2 * q + s, :, :, :], src, ACT.Copy, t, state["arena"])
                else:
                    e = dve(lambda en, s=s, src=src: en.tensor_copy(W1[:, 2 * q + s, :, :, :], src), t,
                            state["arena"])
                w1.append(e)
            bfree[i] = w1[-2:]
            return t

        read = {}

        def beside_v(k):
            if 0 < k < 5:
                turn_u(2 * k - 2)
                read["u2"] = turn_u(2 * k - 1)
            if k == 5:
                read["big"] = s5_big2(read["u2"])
            if k > 0:
                turn_w(k - 1)
            if k > 5:
                next(read["big"])

        banks, t = gemm_tokens(lambda h, k, m: h[:, k, m * P:(m + 1) * P], hw, beside_v)
        vt = []
        for m in range(4):
            e = A(Vt[:, m, :], bank_t[banks[m]][:, :], ACT.Copy, t, rc, state["arena"], scale=rcol[:, m:m + 1])
            bfree[banks[m]] = [e]
            vt.append(e)
        state["rcol_used"] = [state["rcol_used"], e, u2]
        w1_read = turn_w(7)
        big = read["big"]

        def scaled(banks, t, hb):
            for i in range(2):
                qk[hb + i] = [stt(Qf[:, hb + i, :], bank_t[banks[i]][:, :], 0.125, Rb[:, :], MUL, MUL, t, rb,
                                  state["arena"]),
                              tt(dve, Kf[:, hb + i, :], bank_t[banks[2 + i]][:, :], Rb[:, :], MUL, t, rb,
                                 state["arena"])]
                bfree[banks[i]], bfree[banks[2 + i]] = qk[hb + i][:1], qk[hb + i][1:]
            state["Rb_used"] = qk[hb + 1]

        fs = []

        def inputs(q):
            i, b, w0 = bank()
            for g8 in range(8):
                g = 8 * q + g8
                t = mm(b[:, g8 * 64:(g8 + 1) * 64], W1[:, g // 2, g % 2, :, :], Up[:, g, :], True, True, w1, ups, w0,
                       sig=g8 == 7, skip=True)
            v4 = b[:, :].rearrange("p (a g j) -> p a g j", a=4, g=2)
            ev = []
            for g2 in range(2):
                for ri in range(2):
                    dst = FS[64 * g2:64 * g2 + 64, :, ri, 4 * q:4 * q + 4].rearrange("p j a -> p a j")
                    src = v4[64 * ri:64 * ri + 64, :, g2, :]
                    if ri == 0:
                        ev.append(A(dst, src, ACT.Copy, t, w1_read))
                    else:
                        ev.append(dve(lambda en, dst=dst, src=src: en.tensor_copy(dst, src), t, w1_read))
            bfree[i] = ev
            fs.extend(ev)
            read["w1"] = t

        def beside_qk(k):
            if k < 4:
                inputs(k)
                next(big, None)

        qk = {}
        banks, t = gemm_group(Hh, Hl, hw, beside_qk)
        g_in = state["g_in"]
        scaled(banks, t, 0)
        w3z = pool(lambda e: e.memset(W3[:, :, :], 0.0), g_in)
        x0 = pool(lambda e: e.memset(XS[:, 0, :, :], 0.0), w1_read)
        xw = x0
        M = M8[:, :, :]
        st = small[:, 0:64].rearrange("p (a b) -> p a b", a=2)
        sx = state.get("small_used")
        for j in range(63):
            xj = XS[:, j, :, :].rearrange("p a b -> p (a b)").unsqueeze(1).to_broadcast([P, 2, 32])
            a = pool(lambda e, xj=xj: e.tensor_tensor(st, xj, M, MUL), xw, fs, s5_in, sx)
            b_ = pool(lambda e, j=j: e.tensor_tensor(XS[:, j + 1, :, :], st[:, :, 0:16], FS[:, j, :, :], ADD), a)
            xw = pool(lambda e, j=j: e.tensor_tensor(XS[:, j + 1, :, :], XS[:, j + 1, :, :], st[:, :, 16:32], ADD), b_)
        state["small_used"] = xw

        kr = []

        def lags(q):
            i, b, w0 = bank()
            par = q % 2
            for s in range(4):
                o = b[0:16, s * P:(s + 1) * P]
                pr = 4 * (q // 2) + s
                g = 2 * pr + par
                t = mm(o, B2[:, 16 * g:16 * g + 16], G2[:, g, 0:8, :], True, True, g_in, b2_in, w0, read["w1"],
                       sig=s == 3, skip=True)
            e = A(Kr[0:16, 8 * (q // 2) + par:8 * (q // 2) + 8:2, :], b[0:16, :].rearrange("p (s n) -> p s n", s=4),
                  ACT.Copy, t, read["w1"])
            bfree[i] = [e]
            kr.append(e)

        sp(lambda en: en.dma_start(Dp[:, :], att_d[:, 0, :]), state["zsum_used"], sig=sem["s_att"])
        sp(lambda en: en.dma_start(Cn[:, :], att_d[:, 1, :]), g_in, sig=sem["s_att"])
        att_in = (sem["s_att"], 32)
        units = [(h, tb) for h in range(HEADS) for tb in range(4)]
        at = {}
        ptw = []
        mw = []
        early = []

        def scores(u):
            h, tb = units[u]
            r = slice(64 * (h % 2), 64 * (h % 2) + 64)
            n = P * (tb + 1)
            i, b, w0 = bank()
            t = mm(b[:, 0:n], Qf[r, h // 2, tb * P:(tb + 1) * P], Kf[r, h // 2, 0:n], True, True, qk[h // 2], w0, sig=True)
            s, o = tmp[u % 4], 32 + 4 * (u % 4)
            s1 = stt(s[:, 0:n], Dp[:, T - n:T], -2.0 ** -(h + 1), b[:, 0:n], MUL, ADD, t, att_in, state["tmp"][u % 4])
            bfree[i] = [s1]
            mx = dve(lambda e: e.tensor_reduce(rcol[:, o:o + 1], s[:, 0:n], AX_X, ALU.max, negate=True), s1,
                     state["rcol_used"] if u < 4 else at[u - 4])
            at[u] = A(s[:, 0:n], s[:, 0:n], ACT.Exp, mx, bias=rcol[:, o:o + 1])

        def weights(u):
            h, tb = units[u]
            n = P * (tb + 1)
            s, o = tmp[u % 4], 32 + 4 * (u % 4)
            pc = stt(s[:, 0:n], s[:, 0:n], 1.0, Cn[:, T - n:T], MUL, MUL, at[u], accum_out=rcol[:, o + 1:o + 2])
            rd = dve(lambda e: e.reciprocal(rcol[:, o + 2:o + 3], rcol[:, o + 1:o + 2]), pc)
            at[u] = A(s[:, 0:n], s[:, 0:n], ACT.Copy, rd, scale=rcol[:, o + 2:o + 3])

        def turn(u):
            h, tb = units[u]
            n = P * (tb + 1)
            i, b, w0 = bank()
            for sb in range(tb + 1):
                t = tr(b[:, sb * P:(sb + 1) * P], tmp[u % 4][:, sb * P:(sb + 1) * P], ident, at[u], w0, sig=sb == tb)
            state["tmp"][u % 4] = t
            e = dve(lambda en: en.tensor_copy(
                PT[:, 0:tb + 1, tb * P:(tb + 1) * P], b[:, 0:n].rearrange("p (s t) -> p s t", t=P)),
                t, state.get("pt_used"), w_in, g_in, state["arena"])
            bfree[i] = [e]
            ptw.append(e)

        def values(h):
            hb = h // 2
            r = slice(64 * (h % 2), 64 * (h % 2) + 64)
            if h % 2 == 0:
                state["ob"] = bank()
            i, b, w0 = state["ob"]
            for sb in range(4):
                t = mm(b[r, sb * P:T], Vt[:, sb, 64 * h:64 * h + 64], PT[:, sb, sb * P:T], sb == 0, sb == 3, vt,
                       ptw[4 * h:4 * h + 4], w0, sig=sb == 3)
            state["pt_used"] = t
            if h in (1, 3):
                early.append(A(Qf[:, hb, :], b[:, :], ACT.Copy, t))
                bfree[i] = early[-1:]
            elif h % 2:
                split_o(hb, b[:, :], t)
                bfree[i] = mw[hb]

        rests = []

        def split_o(hb, src, ready):
            parts = [A(Hh[:, hb, :], src, ACT.Copy, ready, state["h_used"])]
            mw.append(parts)
            rests.append(lambda: parts.append(
                tt(dve, Hl[:, hb, :], src, f32(Hh[:, hb, :]), SUB, parts[0], ready, state["h_used"])))

        def attention():
            for u in range(-3, len(units)):
                begun = len(rests)
                if 0 <= u + 1 < len(units):
                    weights(u + 1)
                if u + 3 < len(units):
                    scores(u + 3)
                if u > 0 and u % 4 == 0:
                    values(u // 4 - 1)
                if u >= 0:
                    turn(u)
                for _ in range(begun):
                    rests.pop(0)()
                yield u
            values(HEADS - 1)
            while rests:
                rests.pop(0)()

        def beside_qk2(k):
            for _ in range(2):
                next(heads)

        heads = attention()
        banks, t = gemm_group(Hh, Hl, hw, beside_qk2)
        state["h_used"] = t
        scaled(banks, t, 2)
        def with_skip():
            dsk = tmp[4][0:16, :].rearrange("p (g n) -> p g n", n=16)
            e = tt(dve, dsk, ident[0:16, 0:16].unsqueeze(1).to_broadcast([16, 32, 16]),
                   c("d_skip")[0:16, :].unsqueeze(2).to_broadcast([16, 32, 16]), MUL, state["tmp"][4], cst_in)
            e = tt(dve, Kr[0:16, :, 0:16], Kr[0:16, :, 0:16], dsk, ADD, e, kr)
            state["tmp"][4] = e
            for m in range(8):
                sp(lambda en, m=m: en.dma_start(W3[16 * m:16 * m + 16, :, 16 * m:P], Kr[0:16, :, 0:P - 16 * m]), e, w3z,
                   sig=sem["s_w3"])

        w3_in = (sem["s_w3"], 16 * 8)
        def s5_out():
            xs2 = []
            for g2 in range(2):
                for ri in range(2):
                    dst = XS2[64 * ri:64 * ri + 64, :, g2:32:2]
                    src = XS[64 * g2:64 * g2 + 64, :, ri, :]
                    if ri == g2:
                        xs2.append(A(dst, src, ACT.Copy, xw))
                    else:
                        xs2.append(dve(lambda en, dst=dst, src=src: en.tensor_copy(dst, src), xw))
            yield
            y2 = []
            for q in range(8):
                i, b, w0 = bank()
                par = q % 2
                for s in range(4):
                    pr = 4 * (q // 2) + s
                    g = 2 * pr + par
                    o = b[0:64, s * P:(s + 1) * P]
                    mm(o, Up[:, g, :], W3[:, g, :], True, False, w3_in, w0, skip=True)
                    t = mm(o, XS2[:, :, g], G2[:, g, 1:9, :], False, True, xs2, sig=s == 3, skip=True)
                src = b[0:64, :].rearrange("p (s t n) -> p s t n", s=4, t=8)
                g0 = 8 * (q // 2) + par
                dst = Y2[0:64, :, :].rearrange("p t (g n) -> p g t n", n=16)[:, g0:g0 + 7:2, :, :]
                if q % 2:
                    e = A(dst, src, ACT.Copy, t, w3_in)
                else:
                    e = dve(lambda en, dst=dst, src=src: en.tensor_copy(dst, src), t, w3_in)
                bfree[i] = [e]
                y2.append(e)
                yield
            mats_read = t
            for cb in range(4):
                i, b, w0 = bank()
                for tt_ in range(8):
                    t = tr(b[:, tt_ * 64:(tt_ + 1) * 64], Y2[0:64, tt_, P * cb:P * (cb + 1)], ident[0:64, 0:64], y2, w0,
                           sig=tt_ == 7)
                g = A(yg[:, cb, :].rearrange("p (j t) -> p t j", t=8), b[:, :].rearrange("p (t j) -> p t j", t=8),
                      ACT.Gelu_apprx_tanh, t, mats_read)
                bfree[i] = [g]
                hi = A(yh[:, cb, :], yg[:, cb, :], ACT.Copy, g, mats_read)
                lo = tt(dve, yl[:, cb, :], yg[:, cb, :], f32(yh[:, cb, :]), SUB, hi, mats_read)
                yw.append([hi, lo])

        yw = []
        ssm = s5_out()
        for u in heads:
            if len(kr) < 8:
                lags(len(kr))
                if len(kr) == 8:
                    with_skip()
            if u == 16:
                for hb in range(2):
                    split_o(hb, Qf[:, hb, :], early[hb])
            if u >= 23:
                next(ssm, None)
        for _ in ssm:
            pass
        late[0] = False
        held = half_rows(Hh, Hl, mw)
        for nb in range(4):
            i, t = gemm_row(4, yh, yl, yw)
            s = A(tmp[nb][:, :], bank_t[i][:, :], ACT.Sigmoid, t, state["tmp"][nb], cst_in, bias=c("b_glu", nb))
            bfree[i] = [s]
            m = tt(dve, tmp[nb][:, :], tmp[nb][:, :], yg[:, nb, :], MUL, s)
            hi = A(Hh[:, 4 + nb, :], tmp[nb][:, :], ACT.Copy, m, state["h_used"])
            lo = tt(dve, Hl[:, 4 + nb, :], tmp[nb][:, :], f32(Hh[:, 4 + nb, :]), SUB, hi, state["h_used"])
            state["tmp"][nb] = lo
            mw.append([hi, lo])
        state["zsum_used"] = state["MUb_used"] = lo
        state["arena"] = [t, lo]
        state["y_free"] = None
        ycp, t = out_rms(KD, Hh, Hl, mw, held)
        state["h_used"] = t
        return post_norm(lambda k: c("g_mpost", k), ycp, lambda k, x: pre_norm("g_f2pre", k, x))

    def mixer_2(l, hw):
        af = state["arena"]
        lb_in, msk_in = state["lb_in"], state["msk_in"]
        zs = pool(lambda e: e.memset(Sc[:, :, :, :], 0.0), af)
        zp = pool(lambda e: e.memset(U3[:, :, 0:16], 0.0), af)
        zp = pool(lambda e: e.memset(PA[:, :, 0:16], 0.0), af)
        banks, t = gemm_group(Hh, Hl, hw)
        ft, ks = [], []
        for h in range(4):
            b = bank_t[banks[h]]
            s = A(FT[:, h, :], b[:, :], ACT.Sigmoid, t, af)
            s2 = A(KS[:, h, :], b[:, :], ACT.Sigmoid, t, af, scale=-1.0)
            bfree[banks[h]] = [s2]
            ft.append(ts(dve, FT[:, h, :], FT[:, h, :], hcol[:, 8 + 4 * l + h:9 + 4 * l + h],
                         hcol[:, 4 * l + h:4 * l + h + 1], MUL, ADD, s, lb_in))
            ks.append(ts(dve, KS[:, h, :], KS[:, h, :], hcol[:, 8 + 4 * l + h:9 + 4 * l + h], None, MUL, None, s2, lb_in))
        banks, t = gemm_group(Hh, Hl, hw)
        later.pop()()
        qp = []
        for h in range(4):
            e = A(QP[:, h, :], bank_t[banks[h]][:, :], ACT.Copy, t, af, scale=P ** -0.5)
            bfree[banks[h]] = [e]
            qp.append(e)

        flat4 = QP[:, :, :].rearrange("p h t -> p (h t)")
        kflat = KS[:, :, :].rearrange("p h t -> p (h t)")
        fflat = FT[:, :, :].rearrange("p h t -> p (h t)")
        cur = {"q": qp, "k": ks, "t": [ft], "T": fflat, "toff": 0, "used": None, "sw": []}

        def decays(n):
            if n == 0:
                return
            if n == 1:
                cur["q"] = [tt(dve, flat4, flat4, fflat, MUL, cur["q"], ft, cur["used"])]
                return
            m = n // 2
            nb = 4 * T // n
            Tm = cur["T"].rearrange("p (b s) -> p b s", s=2)
            q4 = flat4.rearrange("p (b s i) -> p b s i", s=2, i=m)
            k4 = kflat.rearrange("p (b s i) -> p b s i", s=2, i=m)
            left = Tm[:, :, 0:1].to_broadcast([P, nb, m])
            right = Tm[:, :, 1:2].to_broadcast([P, nb, m])
            q = tt(dve, q4[:, :, 1, :], q4[:, :, 1, :], left, MUL, cur["q"], cur["t"], cur["used"])
            k = tt(pool, k4[:, :, 0, :], k4[:, :, 0, :], right, MUL, cur["k"], cur["t"], cur["used"])
            o = cur["toff"]
            tn = TT[:, o:o + nb]
            t_ = tt(pool, tn, Tm[:, :, 0], Tm[:, :, 1], MUL, cur["t"], af)
            cur.update(q=[q], k=[k], t=[t_], T=tn, toff=o + nb)

        def level(li):
            sw = []
            for h in range(4):
                i, b, w0 = bank()
                for m in range(4):
                    s = slice(m * P, (m + 1) * P)
                    t = mm(b[:, s], KS[:, h, s], QP[:, h, s], True, True, cur["q"], cur["k"], w0, sig=m == 3, skip=True)
                dst = Sc[:, h, :, :].rearrange("p i t -> p (i t)")
                view = bass.AP(tensor=dst.tensor, offset=dst.offset, ap=[list(dst.ap[0]), [640, 4], [1, P]])
                mk = msk[:, li, :].unsqueeze(1).to_broadcast([P, 4, P])
                src = b[:, :].rearrange("p (i t) -> p i t", i=4)
                e = dve(lambda en, view=view, mk=mk, src=src: en.copy_predicated(view, mk, src), t, zs, msk_in,
                        cur["sw"][h] if cur["sw"] else None)
                bfree[i] = [e]
                sw.append(e)
            cur["used"] = t
            cur["sw"] = sw
            decays((LEVELS + (128,))[li + 1])

        def far(n):
            for h in range(4):
                i, b, w0 = bank()
                if n == P:
                    for a in range(2):
                        s, d = slice(2 * a * P, (2 * a + 1) * P), slice((2 * a + 1) * P, (2 * a + 2) * P)
                        t = mm(b[:, a * P:(a + 1) * P], KS[:, h, s], QP[:, h, d], True, True, cur["q"], cur["k"], w0,
                               sig=a == 1, skip=True)
                    e1 = A(Sc[:, h, 0, P:2 * P], b[:, 0:P], ACT.Copy, t, zs)
                    e2 = A(Sc[:, h, 2, 3 * P:4 * P], b[:, P:2 * P], ACT.Copy, t, zs)
                    cur.setdefault("far", []).extend([e1, e2])
                else:
                    for a in range(2):
                        t = mm(b[:, a * 256:(a + 1) * 256], KS[:, h, a * P:(a + 1) * P], QP[:, h, 256:512], True, True,
                               cur["q"], cur["k"], w0, sig=a == 1, skip=True)
                    e2 = A(Sc[:, h, 0:2, 256:512], b[:, :].rearrange("p (a t) -> p a t", a=2), ACT.Copy, t, zs)
                    cur["far"].append(e2)
                bfree[i] = [e2]
            cur["used"] = t
            if n == P:
                decays(256)

        def outputs(h):
            i, b, w0 = bank()
            for m in range(4):
                t = mm(b[:, m * P:T], V2[:, m, h * P:(h + 1) * P], Sc[:, h, m, m * P:T], m == 0, m == 3, vt, cur["sw"],
                       cur["far"], w0, sig=m == 3)
            s, used = ((acc, "acc_used"), (zsum, "zsum_used"))[h % 2]
            e1 = A(Oh[:, h, :], b[:, :], ACT.Copy, t, af)
            e2 = A(s[:, :], b[:, :], ACT.Square, t, state[used])
            bfree[i] = [e2]
            oh.append([e1, e2])

        def head_cols(h):
            s, used = ((acc, "acc_used"), (zsum, "zsum_used"))[h % 2]
            i, b, w0 = bank()
            zero_cols(b, w0)
            t = col_sums(s[:, :], b, 0, oh[h][1])
            state[used] = t
            e = A(small[:, 4 * h:4 * h + 4], b[:, 0:8:2], ACT.Sqrt, t, eps_in, state.get("small_used"), scale=1.0 / P,
                  bias=epsc[:, 0:1])
            bfree[i] = [e]
            rc.append(dve(lambda en: en.reciprocal(rcol[:, 4 * h:4 * h + 4], small[:, 4 * h:4 * h + 4]), e,
                          state["rcol_used"]))
            made.append(spread_cols(rcol[:, 4 * h:4 * h + 4], rc[h], 2 + h))

        def head_norm(h):
            i, b, w0 = bank()
            t, dg = spread_mm(made[h], b, w0)
            oh[h] = tt(dve, Oh[:, h, :], Oh[:, h, :], b[:, :], MUL, t, oh[h])
            bfree[i] = [oh[h]]
            if h == 3:
                state["small_used"] = rc[h]
                state["rcol_used"] = dg

        def pooled(g):
            w = 2 << g
            src, sw_ = U3[:, g, :], ug[g]
            d = 1
            n = 0
            while d < w:
                dst = PA[:, n % 2, :]
                sw_ = tt(pool, dst[:, 16:16 + T], src[:, 16:16 + T], src[:, 16 - d:16 - d + T], ADD, sw_, zp,
                         cur.get("pa"))
                src = dst
                d *= 2
                n += 1
            e1 = stt(tmp[g][:, :], src[:, 16:16 + T], 1.0 / w, U3[:, g, 16:16 + T], MUL, SUB, sw_, state["tmp"][g])
            e2 = tt(dve, sq[:, 16 * g:16 * g + 16], src[:, 16:32], c("rcount", 16 * g, 16), MUL, sw_, cst_in,
                    state["sq_used"])
            pl.append(tt(dve, tmp[g][:, 0:16], sq[:, 16 * g:16 * g + 16], U3[:, g, 16:32], SUB, e2, e1))
            cur["pa"] = e2

        def pooled_split(g):
            hi = A(Ph[:, g, :], tmp[g][:, :], ACT.Copy, pl[g], cur["used"])
            lo = tt(dve, Pl[:, g, :], tmp[g][:, :], f32(Ph[:, g, :]), SUB, hi, cur["used"])
            state["tmp"][g] = lo
            pl[g] = [hi, lo]

        oh, rc, pl, made = [], [], [], []
        banks, t = gemm_tokens(lambda h, k, m: h[:, k, m * P:(m + 1) * P], hw,
                               lambda k: level(k // 2) if k % 2 else None)
        vt = []
        for m in range(4):
            e = A(V2[:, m, :], bank_t[banks[m]][:, :], ACT.Copy, t, af)
            bfree[banks[m]] = [e]
            vt.append(e)
        banks, t = gemm_group(Hh, Hl, hw, lambda k: level(4 + k // 2) if k % 2 else None)
        ug = []
        for g in range(4):
            e = A(U3[:, g, 16:16 + T], bank_t[banks[g]][:, :], ACT.Copy, t, af, zp)
            bfree[banks[g]] = [e]
            ug.append(e)

        def beside_g(k):
            if k == 0:
                far(128)
                pooled(0)
                pooled(1)
            elif k == 2:
                far(256)
                pooled(2)
                pooled(3)
            elif k == 3:
                outputs(0)
            elif k == 4:
                outputs(1)
                head_cols(0)
                pooled_split(0)
                pooled_split(1)
            elif k == 5:
                head_norm(0)
                outputs(2)
                head_cols(1)
                pooled_split(2)
                pooled_split(3)
            elif k == 6:
                head_norm(1)
                outputs(3)
                head_cols(2)
            elif k == 7:
                head_norm(2)
                head_cols(3)
                A(epsc[:, 3:4], epsc[:, 0:1], ACT.Silu, eps_in)

        banks, t = gemm_group(Hh, Hl, hw, beside_g)
        state["h_used"] = h_used = t
        mw = [None] * KD
        sg = []
        for h in range(4):
            sg.append(A(Sg[:, h, :], bank_t[banks[h]][:, :], ACT.Silu, h_used, af))
            bfree[banks[h]] = [sg[h]]
        for g in range(4):
            i, b, w0 = bank()
            hi, lo, w, unit = wtile()
            t = mm3(b[:, :], hi, lo, Ph[:, g, :], Pl[:, g, :], True, True, [w, w0], pl[g], unit, sig=True)
            sc = c("pool_scale", 4 * l + g)
            hi = A(Hh[:, g, :], b[:, :], ACT.Copy, t, h_used, scale=sc)
            lo = stt(Hl[:, g, :], b[:, :], sc, f32(Hh[:, g, :]), MUL, SUB, hi, h_used)
            bfree[i] = [hi, lo]
            mw[g] = [hi, lo]
            if g == 0:
                head_norm(3)
        for h in range(4):
            e = stt(tmp[h][:, :], Oh[:, h, :], c("hg", l), Sg[:, h, :], MUL, MUL, sg[h], oh[h], state["tmp"][h], cst_in)
            hi = A(Hh[:, 4 + h, :], tmp[h][:, :], ACT.Copy, e, h_used)
            lo = tt(dve, Hl[:, 4 + h, :], tmp[h][:, :], f32(Hh[:, 4 + h, :]), SUB, hi, h_used)
            state["tmp"][h] = lo
            mw[4 + h] = [hi, lo]
        state["arena"] = [lo, t]
        state["y_free"] = None
        hw, t = out_ln(KD, Hh, Hl, mw, 1.0, 3 * l + 1, held=half_rows(Hh, Hl, mw))
        return hw

    def ffn_1(hw, post_g, then):
        aw = ffn_in(hw, rms_spread())
        state["arena"] = None
        ycp, t = out_rms(NF, Ah, Al, aw)
        hw = post_norm(post_g, ycp, then)
        state["arena"] = [t, state["y_free"]]
        return hw

    def ffn_2(hw, li, last=False):
        aw = ffn_in(hw, None)
        state["arena"] = None
        hw, t = out_ln(NF, Ah, Al, aw, 0.5, li, last)
        state["arena"] = [t, state["y_free"]]
        return hw

    def bounds():
        lb = c("lb")
        d = tt(dve, hcol[:, 16:20], lb[:, 0:4], lb[:, 4:8], ALU.max, cst_in)
        d = tt(dve, hcol[:, 20:24], lb[:, 0:4], hcol[:, 16:20], SUB, d)
        d = tt(dve, hcol[:, 24:28], lb[:, 4:8], hcol[:, 16:20], SUB, d)
        e = A(hcol[:, 20:28], hcol[:, 20:28], ACT.Exp, d)
        yield
        d = tt(dve, hcol[:, 16:20], hcol[:, 20:24], hcol[:, 24:28], ADD, e)
        d = dve(lambda e: e.reciprocal(hcol[:, 28:32], hcol[:, 16:20]), d)
        d = tt(dve, hcol[:, 20:24], hcol[:, 20:24], hcol[:, 28:32], MUL, d)
        d = tt(dve, hcol[:, 24:28], hcol[:, 24:28], hcol[:, 28:32], MUL, d)
        yield
        d = tt(dve, hcol[:, 24:28], hcol[:, 20:24], hcol[:, 24:28], ADD, d)
        d = tt(dve, hcol[:, 0:4], hcol[:, 20:24], hcol[:, 20:24], SUB, d)
        d = tt(dve, hcol[:, 4:8], hcol[:, 24:28], hcol[:, 20:24], SUB, d)
        state["lb_in"] = ts(dve, hcol[:, 8:16], hcol[:, 0:8], -1.0, 1.0, MUL, ADD, d)

    def beside():
        sp(lambda e: e.dma_start(tmp[4][:, :], s5_d[:, 0, :]), state["tmp"][4], sig=sem["s_s5"])
        state["msk_in"] = dve(lambda e: e.tensor_copy(msk[:, :, :].rearrange("p a b -> p (a b)"),
                                                      Y[:, 0:2, :].rearrange("p a b -> p (a b)")), (sem["s_msk"], 16))
        state["y_free"] = state["msk_in"]
        yield
        yield from s5_small()
        yield
        yield from bounds()

    side = beside()
    prep(0)
    hw = []
    for k in range(KD):
        hw.append(pre_norm("g_f1pre", k, state["x"][k]))
        if k == 1:
            prep(1)
    hw = ffn_1(hw, lambda k: gh[:, k:k + 1], lambda k, x: pre_norm("g_mpre", k, x))
    hw = mixer_1(hw)

    def no_norm(k, x):
        return split_h(k, X[:, k, :], None, x)

    hw = ffn_1(hw, lambda k: gh[:, 8 + k:9 + k], no_norm)
    later.append(lambda hw=hw: scale_x(hw))
    for _ in side:
        pass
    for l in range(2):
        hw = ffn_2(hw, 3 * l)
        hw = mixer_2(l, hw)
        hw = ffn_2(hw, 3 * l + 2, last=l == 1)
    assert pos[0] == n_units * 8, (pos[0], n_units)
    sp(lambda e: e.wait_ge(sem["s_out"], 16 * KD), sig=False)

    with nc.Block() as block:
        @block.sync
        def _(eng):
            run_queue(eng, sp)

        @block.tensor
        def _(eng):
            run_queue(eng, pe)

        @block.scalar
        def _(eng):
            run_queue(eng, act)

        @block.vector
        def _(eng):
            run_queue(eng, dve)

        @block.gpsimd
        def _(eng):
            run_queue(eng, pool)


def attention_tables():
    import numpy as np

    t = np.arange(P)[:, None]
    s = np.arange(T)[None, :] - 3 * P
    dist = t - s
    count = np.zeros(dist.shape, np.float32)
    for window, dilation in ((128, 1), (512, 4), (2048, 16)):
        count += (dist >= 0) & (dist <= window) & (dist % dilation == 0)
    far = np.where(count > 0, dist, 1e30).astype(np.float32)
    return np.stack([far, count], 1)


def level_masks():
    import numpy as np

    s, t = np.arange(P)[:, None], np.arange(P)[None, :]
    masks = [s == t]
    for n in LEVELS[1:]:
        masks.append((s // (2 * n) == t // (2 * n)) & (s // n % 2 == 0) & (t // n % 2 == 1))
    return np.stack(masks, 1).astype(np.float32).reshape(P, 2, 512)


def kernel(**inputs):
    import numpy as np
    import concourse.bacc as bacc
    from concourse.bass_utils import run_bass_kernel_spmd

    a = {k: np.asarray(v) for k, v in inputs.items()}

    def tiles(w):
        k, n = w.shape
        return w.reshape(k // P, P, n // P, P).transpose(0, 2, 1, 3)

    mats = {"f1_in": tiles(a["ffn1_w_in"][0]), "f1_out": tiles(a["ffn1_w_out"][0]), "mix_in": tiles(a["w_mix_in"][0]),
            "glu": tiles(a["w_glu"][0]), "mix_out": tiles(a["w_mix_out"][0]), "f2_in": tiles(a["ffn2_w_in"][0]),
            "f2_out": tiles(a["ffn2_w_out"][0])}
    for l in range(2):
        for n in (1, 2):
            mats[f"gate{n}_{l}"] = tiles(a[f"ffn{n}_gate_2"][l])
            mats[f"up{n}_{l}"] = tiles(a[f"ffn{n}_up_2"][l])
            mats[f"down{n}_{l}"] = tiles(a[f"ffn{n}_down_2"][l])
        mats[f"in_{l}"] = tiles(a["w_in_2"][l])
        mats[f"out_{l}"] = tiles(a["w_out_2"][l])
        for g in range(4):
            mats[f"pool{g}_{l}"] = tiles(a["pool_w_2"][l, g])
    plan = stream_plan()
    assert len(plan) % 8 == 0
    stream = np.empty((len(plan) // 8, P, 8, P), np.float32)
    for i, (name, k, n) in enumerate(plan):
        stream[i // 8, :, i % 8, :] = mats[name][k, n]
    stream = stream.reshape(len(plan) // 8, P, 8 * P)

    def cols(v, n):
        return v.reshape(n, P).T

    def pairs(v):
        v = v.reshape((16, 2, 64) + v.shape[2:])
        return np.moveaxis(v, 0, 2).reshape((P, 16) + v.shape[3:])

    cst = np.zeros((P, NCOLS), np.float32)

    def put(name, v):
        cst[:v.shape[0], COLS[name][0]:COLS[name][1]] = v

    put("ident", np.eye(P, dtype=np.float32))
    for name, key in (("g_f1pre", "ffn1_pre_g"), ("g_f1post", "ffn1_post_g"), ("g_mpre", "mix_pre_g"),
                      ("g_mpost", "mix_post_g"), ("g_f2pre", "ffn2_pre_g"), ("g_f2post", "ffn2_post_g")):
        put(name, cols(a[key], 8))
    put("ln_g", cols(a["ln_g_2"], 48))
    put("ln_b", cols(a["ln_b_2"], 48))
    put("pool_scale", cols(a["pool_scale_2"], 8))
    put("lb", cols(a["lb_param_2"], 8))
    put("hg", cols(a["hgrn_norm_g_2"], 2))
    put("b_glu", cols(a["b_glu"], 4))
    put("a_re", pairs(a["a_re"][0]))
    put("a_im", pairs(a["a_im"][0]))
    put("log_dt", pairs(np.broadcast_to(a["log_dt"][0][:, None], (32, 64))))
    put("d_skip", a["d_skip"].reshape(32, 16).T)
    pos = np.arange(16)
    put("rcount", np.broadcast_to(np.concatenate(
        [1.0 / np.minimum(pos + 1, w) for w in (2, 4, 8, 16)]).astype(np.float32), (P, 64)))
    s5 = np.concatenate([pairs(a["b_re"][0]).reshape(P, 256), pairs(a["b_im"][0]).reshape(P, 256),
                         pairs(a["c_re"][0].transpose(0, 2, 1)).reshape(P, 256),
                         pairs(a["c_im"][0].transpose(0, 2, 1)).reshape(P, 256)], 1).reshape(P, 2, 512)
    x = a["x"][0].T.reshape(KD, P, T).transpose(1, 0, 2)
    arrays = {"x_t": x, "weights": stream, "vectors": cst, "ssm": s5, "attention": attention_tables(),
              "masks": level_masks()}
    arrays = {k: np.ascontiguousarray(v) for k, v in arrays.items()}

    nc = bacc.Bacc("TRN2", target_bir_lowering=False, num_devices=1, dynamic_dma_scratch_size=1024)
    args = [nc.dram_tensor(k, v.shape, mybir.dt.from_np(v.dtype), kind="ExternalInput").ap() for k, v in arrays.items()]
    out = nc.dram_tensor("y_t", (P, KD, T), F32, kind="ExternalOutput").ap()
    build(nc, *args, out)
    r = run_bass_kernel_spmd(nc, [arrays], core_ids=[0])
    y = np.asarray(r.results[0]["y_t"])
    return y.transpose(1, 0, 2).reshape(D, T).T[None].copy()
```
